# Optimizing a Trainium2 kernel written in Bass

```python
import math
import jax, jax.numpy as jnp
from jax import lax
import numpy as np

D_MODEL = 2048
BATCH = 1
SEQ = 512
DEPTH = 1
DEC_BATCH = 8
DEC_SEQ = 4
PAST_LEN = 1024
PAGE_SIZE = 128

N_HEADS = 8
HEAD_DK = 64
HEAD_DV = 2 * HEAD_DK
QK_COLS = N_HEADS * 2 * HEAD_DK
ATTN_WIDTH = N_HEADS * HEAD_DV
ROPE_DIMS = HEAD_DK // 4
ROPE_THETA = 500000.0
Q_BLOCK = 128
NEG_INF = -1e30
SSM_WIDTH = D_MODEL // 2
SSM_GROUP = 16
SSM_GROUPS = SSM_WIDTH // SSM_GROUP
SSM_STATE = 64
DT_MIN = 1e-3
DT_MAX = 1e-1
PEER_HEADS = 8
PEER_KEYS = 128
PEER_EXPERTS = PEER_KEYS * PEER_KEYS
PEER_DKEY = 256
PEER_TOPK = 16
PEER_BLOCK = 128
PLE_DIM = 256
RMS_EPS = 1e-6
V_END = 2 * QK_COLS + ATTN_WIDTH
U_END = V_END + SSM_WIDTH
IN_COLS = U_END + 2 * D_MODEL

kernel_name = 'diffattn_s5_peer_hybrid_step'

def rmsnorm(x, g):
    xf = x.astype(jnp.float32)
    y = xf * lax.rsqrt(jnp.mean(xf * xf, axis=-1, keepdims=True) + RMS_EPS)
    return y.astype(x.dtype) * g

def partial_rope(x, pos):
    half = ROPE_DIMS // 2
    inv_freq = ROPE_THETA ** (-jnp.arange(half, dtype=jnp.float32) / half)
    ang = pos.astype(jnp.float32)[:, None] * inv_freq[None, :]
    cos = jnp.cos(ang)[None, :, None, None, :]
    sin = jnp.sin(ang)[None, :, None, None, :]
    xf = x.astype(jnp.float32)
    x1, x2 = xf[..., :half], xf[..., half:ROPE_DIMS]
    out = jnp.concatenate([x1 * cos - x2 * sin, x2 * cos + x1 * sin, xf[..., ROPE_DIMS:]], axis=-1)
    return out.astype(x.dtype)

def diff_attention(q, q_pos, segments, lam):
    B, Tq = q.shape[0], q.shape[1]
    qb = min(Q_BLOCK, Tq)
    n_blk = -(-Tq // qb)
    pad = n_blk * qb - Tq
    q = jnp.pad(q, ((0, 0), (0, pad), (0, 0), (0, 0), (0, 0)))
    q_pos = jnp.pad(q_pos, (0, pad), mode='edge')
    q_blocks = jnp.moveaxis(q.reshape(B, n_blk, qb, N_HEADS, 2, HEAD_DK), 1, 0)
    p_blocks = q_pos.reshape(n_blk, qb)
    scale = HEAD_DK ** -0.5

    def one_block(args):
        q_blk, pos_blk = args
        scores = []
        for k, _, k_pos in segments:
            s = jnp.einsum('bqhmd,bkhmd->bhmqk', q_blk, k).astype(jnp.float32) * scale
            scores.append(jnp.where(k_pos[None, :] <= pos_blk[:, None], s, NEG_INF))
        probs = jax.nn.softmax(jnp.concatenate(scores, axis=-1), axis=-1)
        wts = probs[:, :, 0] - lam * probs[:, :, 1]
        outs = []
        off = 0
        for k, v, _ in segments:
            tk = k.shape[1]
            outs.append(jnp.einsum('bhqk,bkhd->bqhd', wts[..., off:off + tk].astype(v.dtype), v))
            off += tk
        return sum(outs)

    out = lax.map(one_block, (q_blocks, p_blocks))
    return jnp.moveaxis(out, 0, 1).reshape(B, n_blk * qb, N_HEADS, HEAD_DV)[:, :Tq]

def _ssm_combine(e1, e2):
    a1r, a1i, b1r, b1i = e1
    a2r, a2i, b2r, b2i = e2
    return (a1r * a2r - a1i * a2i,
            a1r * a2i + a1i * a2r,
            a2r * b1r - a2i * b1i + b2r,
            a2r * b1i + a2i * b1r + b2i)

def s5_scan(u, h0, a_re, a_im, log_dt, b_re, b_im, c_re, c_im, d_skip):
    f32 = jnp.float32
    uf = u.astype(f32)
    a_re, a_im = a_re.astype(f32), a_im.astype(f32)
    dt = jnp.exp(log_dt.astype(f32))[:, None]
    mag = jnp.exp(a_re * dt)
    ab_re, ab_im = mag * jnp.cos(a_im * dt), mag * jnp.sin(a_im * dt)
    den = a_re * a_re + a_im * a_im
    f_re = ((ab_re - 1.0) * a_re + ab_im * a_im) / den
    f_im = (ab_im * a_re - (ab_re - 1.0) * a_im) / den
    b_re, b_im = b_re.astype(f32), b_im.astype(f32)
    bb_re = f_re[..., None] * b_re - f_im[..., None] * b_im
    bb_im = f_re[..., None] * b_im + f_im[..., None] * b_re
    bu_re = jnp.einsum('gpc,btgc->btgp', bb_re, uf)
    bu_im = jnp.einsum('gpc,btgc->btgp', bb_im, uf)
    elems = (jnp.broadcast_to(ab_re, bu_re.shape), jnp.broadcast_to(ab_im, bu_im.shape), bu_re, bu_im)
    a_cum_re, a_cum_im, h_re, h_im = lax.associative_scan(_ssm_combine, elems, axis=1)
    if h0 is not None:
        h0_re = h0[0].astype(f32)[:, None]
        h0_im = h0[1].astype(f32)[:, None]
        h_re, h_im = (h_re + a_cum_re * h0_re - a_cum_im * h0_im,
                      h_im + a_cum_re * h0_im + a_cum_im * h0_re)
    y = (jnp.einsum('btgp,gcp->btgc', h_re, c_re.astype(f32))
         - jnp.einsum('btgp,gcp->btgc', h_im, c_im.astype(f32))
         + d_skip.astype(f32) * uf)
    return y.astype(u.dtype), h_re[:, -1], h_im[:, -1]

def peer_ffn(h, w_query, sub_keys, expert_u, expert_v):
    B, T, D = h.shape
    n = B * T
    xt = h.reshape(n, D)
    q = (xt @ w_query).reshape(n, PEER_HEADS, 2, PEER_DKEY // 2)
    s = jnp.einsum('nhmd,mkd->nhmk', q, sub_keys).astype(jnp.float32)
    sv, si = lax.top_k(s, PEER_TOPK)
    n_cand = PEER_TOPK * PEER_TOPK
    cand = (sv[:, :, 0, :, None] + sv[:, :, 1, None, :]).reshape(n, PEER_HEADS, n_cand)
    cidx = (si[:, :, 0, :, None] * PEER_KEYS + si[:, :, 1, None, :]).reshape(n, PEER_HEADS, n_cand)
    fv, fpos = lax.top_k(cand, PEER_TOPK)
    eidx = jnp.take_along_axis(cidx, fpos, axis=-1)
    gate = jax.nn.softmax(fv, axis=-1).astype(h.dtype)
    blk = min(PEER_BLOCK, n)
    n_blk = -(-n // blk)
    pad = n_blk * blk - n
    xb = jnp.pad(xt, ((0, pad), (0, 0))).reshape(n_blk, blk, D)
    ib = jnp.pad(eidx, ((0, pad), (0, 0), (0, 0))).reshape(n_blk, blk, PEER_HEADS, PEER_TOPK)
    gb = jnp.pad(gate, ((0, pad), (0, 0), (0, 0))).reshape(n_blk, blk, PEER_HEADS, PEER_TOPK)

    def one_block(args):
        x_blk, i_blk, g_blk = args
        act = jax.nn.gelu(jnp.einsum('nd,nhkd->nhk', x_blk, expert_u[i_blk]))
        return jnp.einsum('nhk,nhkd->nd', g_blk * act, expert_v[i_blk])

    out = lax.map(one_block, (xb, ib, gb)).reshape(n_blk * blk, D)[:n]
    return out.reshape(B, T, D)

def decoder_layer(x, p, pos, past, lam_init, g_mix, w_in, g_q, g_k, lambda_q, lambda_k, g_head, w_attn_up,
                  ssm_a_re, ssm_a_im, ssm_log_dt, ssm_b_re, ssm_b_im, ssm_c_re, ssm_c_im, ssm_d,
                  w_glu, w_out, g_ffn, peer_w_query, peer_sub_keys, peer_u, peer_v, g_ple, w_ple, w_ple_gate):
    B, T, _ = x.shape
    h = rmsnorm(x, g_mix)
    z = h @ w_in
    q = z[..., :QK_COLS].reshape(B, T, N_HEADS, 2, HEAD_DK)
    k = z[..., QK_COLS:2 * QK_COLS].reshape(B, T, N_HEADS, 2, HEAD_DK)
    v = z[..., 2 * QK_COLS:V_END].reshape(B, T, N_HEADS, HEAD_DV)
    u = z[..., V_END:U_END].reshape(B, T, SSM_GROUPS, SSM_GROUP)
    gate_a = jax.nn.sigmoid(z[..., U_END:U_END + D_MODEL])
    gate_s = jax.nn.sigmoid(z[..., U_END + D_MODEL:])

    q = partial_rope(rmsnorm(q, g_q), pos)
    k = partial_rope(rmsnorm(k, g_k), pos)
    lq = lambda_q.astype(jnp.float32)
    lk = lambda_k.astype(jnp.float32)
    lam = jnp.exp(jnp.sum(lq[0] * lk[0])) - jnp.exp(jnp.sum(lq[1] * lk[1])) + lam_init
    segments = [(k, v, pos)]
    h0 = None
    if past is not None:
        k_past, v_past, h0 = past
        past_pos = jnp.arange(k_past.shape[1], dtype=jnp.int32)
        segments = [(k_past, v_past, past_pos), (k, v, pos)]
    att = diff_attention(q, pos, segments, lam)
    att = rmsnorm(att, g_head) * (1.0 - lam_init)
    branch_a = att.reshape(B, T, ATTN_WIDTH) @ w_attn_up

    y_ssm, h_re, h_im = s5_scan(u, h0, ssm_a_re, ssm_a_im, ssm_log_dt, ssm_b_re, ssm_b_im,
                                ssm_c_re, ssm_c_im, ssm_d)
    glu = jax.nn.gelu(y_ssm.reshape(B, T, SSM_WIDTH)) @ w_glu
    branch_s = glu[..., :D_MODEL] * jax.nn.sigmoid(glu[..., D_MODEL:])

    x = x + (gate_a * branch_a + gate_s * branch_s) @ w_out
    x = x + peer_ffn(rmsnorm(x, g_ffn), peer_w_query, peer_sub_keys, peer_u, peer_v)
    x = x + (p @ w_ple) * jax.nn.sigmoid(rmsnorm(x, g_ple) @ w_ple_gate)
    return x, k.reshape(B, T, N_HEADS, 2 * HEAD_DK), v, h_re, h_im

def setup_inputs(seed: int = 0) -> dict:
    key = jax.random.key(seed)
    keys = iter(jax.random.split(key, 48))

    def nrm(shape, scale):
        return jax.random.normal(next(keys), shape, jnp.float32) * scale

    def gain(shape):
        return 1.0 + nrm(shape, 0.05)

    L = DEPTH
    n_pages = PAST_LEN // PAGE_SIZE
    n_used = DEC_BATCH * n_pages
    n_pool = n_used + max(1, n_used // 4)
    page_table = jax.random.permutation(next(keys), n_pool)[:n_used].reshape(DEC_BATCH, n_pages).astype(jnp.int32)
    a_im_base = jnp.pi * jnp.arange(SSM_STATE, dtype=jnp.float32)
    return {
        'x_prompt': nrm((BATCH, SEQ, D_MODEL), 1.0),
        'x_sample': nrm((DEC_BATCH, DEC_SEQ, D_MODEL), 1.0),
        'cache_k': nrm((L, n_pool, PAGE_SIZE, N_HEADS, 2 * HEAD_DK), 1.0),
        'cache_v': nrm((L, n_pool, PAGE_SIZE, N_HEADS, HEAD_DV), 1.0),
        'state_ssm_re': nrm((L, DEC_BATCH, SSM_GROUPS, SSM_STATE), 0.1),
        'state_ssm_im': nrm((L, DEC_BATCH, SSM_GROUPS, SSM_STATE), 0.1),
        'page_table': page_table,
        'p_prompt': nrm((L, BATCH, SEQ, PLE_DIM), 1.0),
        'p_sample': nrm((L, DEC_BATCH, DEC_SEQ, PLE_DIM), 1.0),
        'g_mix': gain((L, D_MODEL)),
        'w_in': nrm((L, D_MODEL, IN_COLS), D_MODEL ** -0.5),
        'g_q': gain((L, 2, HEAD_DK)),
        'g_k': gain((L, 2, HEAD_DK)),
        'lambda_q': nrm((L, 2, HEAD_DK), 0.1),
        'lambda_k': nrm((L, 2, HEAD_DK), 0.1),
        'g_head': gain((L, HEAD_DV)),
        'w_attn_up': nrm((L, ATTN_WIDTH, D_MODEL), ATTN_WIDTH ** -0.5),
        'ssm_a_re': -0.5 + nrm((L, SSM_GROUPS, SSM_STATE), 0.01),
        'ssm_a_im': a_im_base + nrm((L, SSM_GROUPS, SSM_STATE), 0.01),
        'ssm_log_dt': jax.random.uniform(next(keys), (L, SSM_GROUPS), jnp.float32,
                                         math.log(DT_MIN), math.log(DT_MAX)),
        'ssm_b_re': nrm((L, SSM_GROUPS, SSM_STATE, SSM_GROUP), (2 * SSM_GROUP) ** -0.5),
        'ssm_b_im': nrm((L, SSM_GROUPS, SSM_STATE, SSM_GROUP), (2 * SSM_GROUP) ** -0.5),
        'ssm_c_re': nrm((L, SSM_GROUPS, SSM_GROUP, SSM_STATE), SSM_STATE ** -0.5),
        'ssm_c_im': nrm((L, SSM_GROUPS, SSM_GROUP, SSM_STATE), SSM_STATE ** -0.5),
        'ssm_d': nrm((L, SSM_GROUPS, SSM_GROUP), 1.0),
        'w_glu': nrm((L, SSM_WIDTH, 2 * D_MODEL), SSM_WIDTH ** -0.5),
        'w_out': nrm((L, D_MODEL, D_MODEL), D_MODEL ** -0.5),
        'g_ffn': gain((L, D_MODEL)),
        'peer_w_query': nrm((L, D_MODEL, PEER_HEADS * PEER_DKEY), D_MODEL ** -0.5),
        'peer_sub_keys': nrm((L, 2, PEER_KEYS, PEER_DKEY // 2), (PEER_DKEY // 2) ** -0.5),
        'peer_u': nrm((L, PEER_EXPERTS, D_MODEL), D_MODEL ** -0.5),
        'peer_v': nrm((L, PEER_EXPERTS, D_MODEL), PEER_TOPK ** -0.5),
        'g_ple': gain((L, D_MODEL)),
        'w_ple': nrm((L, PLE_DIM, D_MODEL), PLE_DIM ** -0.5),
        'w_ple_gate': nrm((L, D_MODEL, D_MODEL), D_MODEL ** -0.5),
    }

def reference(x_prompt, x_sample, cache_k, cache_v, state_ssm_re, state_ssm_im, page_table, p_prompt, p_sample,
              g_mix, w_in, g_q, g_k, lambda_q, lambda_k, g_head, w_attn_up,
              ssm_a_re, ssm_a_im, ssm_log_dt, ssm_b_re, ssm_b_im, ssm_c_re, ssm_c_im, ssm_d,
              w_glu, w_out, g_ffn, peer_w_query, peer_sub_keys, peer_u, peer_v, g_ple, w_ple, w_ple_gate):
    n_dec = x_sample.shape[0]
    past_len = page_table.shape[1] * PAGE_SIZE
    pos_prompt = jnp.arange(x_prompt.shape[1], dtype=jnp.int32)
    pos_sample = past_len + jnp.arange(x_sample.shape[1], dtype=jnp.int32)
    layer_weights = (g_mix, w_in, g_q, g_k, lambda_q, lambda_k, g_head, w_attn_up,
                     ssm_a_re, ssm_a_im, ssm_log_dt, ssm_b_re, ssm_b_im, ssm_c_re, ssm_c_im, ssm_d,
                     w_glu, w_out, g_ffn, peer_w_query, peer_sub_keys, peer_u, peer_v, g_ple, w_ple, w_ple_gate)
    y_prompt, y_sample = x_prompt, x_sample
    kp, vp, srp, sip, ks, vs, srs, sis = [], [], [], [], [], [], [], []
    for i in range(DEPTH):
        lw = [w[i] for w in layer_weights]
        lam_init = 0.8 - 0.6 * math.exp(-0.3 * i)
        y_prompt, k_new, v_new, h_re, h_im = decoder_layer(y_prompt, p_prompt[i], pos_prompt, None, lam_init, *lw)
        kp.append(k_new); vp.append(v_new); srp.append(h_re); sip.append(h_im)
        k_past = cache_k[i, page_table].reshape(n_dec, past_len, N_HEADS, 2, HEAD_DK)
        v_past = cache_v[i, page_table].reshape(n_dec, past_len, N_HEADS, HEAD_DV)
        past = (k_past, v_past, (state_ssm_re[i], state_ssm_im[i]))
        y_sample, k_new, v_new, h_re, h_im = decoder_layer(y_sample, p_sample[i], pos_sample, past, lam_init, *lw)
        ks.append(k_new); vs.append(v_new); srs.append(h_re); sis.append(h_im)
    return (y_prompt, y_sample,
            jnp.stack(kp), jnp.stack(vp), jnp.stack(srp), jnp.stack(sip),
            jnp.stack(ks), jnp.stack(vs), jnp.stack(srs), jnp.stack(sis))


_drawn_inputs = setup_inputs


def setup_inputs(seed=0):
    import zlib

    import numpy as np

    out = dict(_drawn_inputs(seed))
    spreads = {}
    factors = {'ssm_a_re': 4.338, 'ssm_c_re': 2.7, 'g_ple': 6.402}
    for name, (base, spread) in spreads.items():
        noise = np.random.default_rng([zlib.crc32(name.encode()), seed]).standard_normal(out[name].shape)
        drawn = base * np.exp(spread * noise) if base else spread * noise
        out[name] = __import__('jax').numpy.asarray(drawn.astype(out[name].dtype))
    for name, factor in factors.items():
        out[name] = (out[name] * factor).astype(out[name].dtype)
    return out
```

```python
from contextlib import ExitStack

import numpy as np

import concourse.bass as bass
from concourse import mybir

F32 = mybir.dt.float32
F32R = mybir.dt.float32r
U32 = mybir.dt.uint32
I32 = mybir.dt.int32
ACT = mybir.ActivationFunctionType
ALU = mybir.AluOpType
AX = mybir.AxisListType
ds = bass.ds

P = 128
D_MODEL = 2048
KT = D_MODEL // P
NP = 512
NB, NQ = 8, 4
NS = NB * NQ
TOK = NP + NS
HALF = TOK // 2
NH = 8
DK = 64
DV = 128
PAGE = 128
NPG = 8
PAST = PAGE * NPG
ROPE = DK // 4
G, GC, GS = 64, 16, 64
ST = G // 2
CT = G * GC // P
LO, HI = 32, 16
PK = 128
TOPK = 16
NE = PK * PK
PLE = 256
EPS = 1e-6
LAM_INIT = 0.2
NEG = -1e30
TB = 5
UNIT = 4
RING = 4
PI = float(np.pi)
TWO_PI_A = 6.28125
TWO_PI_B = float(2 * np.pi - 6.28125)
ROUND = 12582912.0

CONST_COLS = [("ident", 128), ("ones", 128), ("block_ones", 128), ("rot", 128), ("causal", 128), ("iota", 128),
              ("cos", TOK), ("sin", TOK), ("pair_sum", NS), ("sample_mask", NQ), ("map_one", 1), ("map_two", 1),
              ("iota16", 16), ("eps", 1)]
CONST_AT = {}
_at = 0
for _name, _w in CONST_COLS:
    CONST_AT[_name] = (_at, _w)
    _at += _w
CONST_W = _at


def shape_constants():
    c = np.zeros((P, CONST_W), np.float32)

    def put(name, value):
        a, w = CONST_AT[name]
        c[:value.shape[0], a:a + w] = value

    put("ident", np.eye(P, dtype=np.float32))
    put("ones", np.ones((P, P), np.float32))
    put("block_ones", np.kron(np.eye(2), np.ones((DK, DK))).astype(np.float32))
    half = ROPE // 2
    rot = np.zeros((P, P), np.float32)
    for m in range(2):
        for j in range(half):
            rot[m * DK + half + j, m * DK + j] = -1.0
            rot[m * DK + j, m * DK + half + j] = 1.0
    put("rot", rot)
    q, k = np.arange(P)[:, None], np.arange(P)[None, :]
    put("causal", np.where(k <= q, 0.0, NEG).astype(np.float32))
    put("iota", np.broadcast_to(np.arange(P, dtype=np.float32), (P, P)))
    put("iota16", np.broadcast_to(np.arange(16, dtype=np.float32), (P, 16)))
    pos = np.concatenate([np.arange(NP), np.tile(PAST + np.arange(NQ), NB)]).astype(np.float32)
    inv = np.float32(500000.0) ** (-np.arange(half, dtype=np.float32) / np.float32(half))
    ang = (pos[None, :] * inv[:, None].astype(np.float32)).astype(np.float32)
    cos, sin = np.ones((P, TOK), np.float32), np.zeros((P, TOK), np.float32)
    for m in range(2):
        for s in range(2):
            cos[m * DK + s * half:m * DK + (s + 1) * half] = np.cos(ang)
            sin[m * DK + s * half:m * DK + (s + 1) * half] = np.sin(ang)
    put("cos", cos)
    put("sin", sin)
    rows = np.arange(2 * NS)
    h, m, t = rows // (2 * NQ), rows // NQ % 2, rows % NQ
    ps = np.zeros((2 * NS, NS), np.float32)
    ps[rows, h * NQ + t] = 1.0
    put("pair_sum", ps)
    put("sample_mask", np.where(np.arange(NQ)[None, :] <= t[:, None], 0.0, NEG).astype(np.float32))
    put("map_one", (m == 0).astype(np.float32)[:, None])
    put("map_two", (m == 1).astype(np.float32)[:, None])
    put("eps", np.full((P, 1), EPS, np.float32))
    return c


class Space:

    def __init__(self, nc, tag):
        self.nc, self.tag, self.stack, self.sems_ = nc, tag, ExitStack(), []

    def __enter__(self):
        return self

    def __exit__(self, *a):
        self.stack.close()
        if self.sems_:
            self.nc.clear_and_free_semaphores(self.sems_)
            self.nc.all_engine_barrier()

    def sb(self, name, shape, dt=F32):
        return self.stack.enter_context(self.nc.sbuf_tensor(f"{self.tag}_{name}", shape, dt))

    def ps(self, name, shape, dt=F32):
        return self.stack.enter_context(self.nc.psum_tensor(f"{self.tag}_{name}", shape, dt))

    def sem(self, name):
        self.sems_.append(self.nc.alloc_semaphore(f"{self.tag}_{name}"))
        return self.sems_[-1]

    def sems(self, name, n):
        return [self.sem(f"{name}{i}") for i in range(n)]

    def block(self):
        return self.stack.enter_context(self.nc.Block())


class Chain:

    def __init__(self, eng, sem):
        self.eng, self.sem, self.n, self.i, self.per, self.k = eng, sem, 0, 0, 0, 0

    def begin(self, i, per):
        self.i, self.per, self.k = i, per, 0

    def end(self, trips):
        assert self.k == self.per, (self.k, self.per)
        self.n, self.i, self.per, self.k = self.n + trips * self.per, 0, 0, 0

    def did(self, ins):
        ins.then_inc(self.sem, 1)
        self.k += 1
        if not self.per:
            self.n, self.k = self.n + 1, 0

    def wait(self):
        self.eng.wait_ge(self.sem, self.i * self.per + (self.n + self.k))

    def step(self, ins):
        self.did(ins)
        self.wait()

    def step_apart(self, ins):
        self.step(ins)
        self.eng.nop(nofuse=True)


def halves(ap):
    return ap.rearrange("p (a n) -> p a n", a=2)


def wide(ap, n):
    return ap.unsqueeze(2).broadcast_to([ap.shape[0], ap.shape[1], n])


def turned(ap, k):
    return ap.unsqueeze(1).broadcast_to([ap.shape[0], k, ap.shape[1]])


class Stream:

    def __init__(self, s):
        self.raw = s.sb("w_raw", [P, RING, UNIT, P])
        self.hi = s.sb("w_hi", [P, RING, UNIT, P], F32R)
        self.rest = s.sb("w_rest", [P, RING, UNIT, P], F32R)
        self.landed = s.sems("w_landed", RING)
        self.hi_done = s.sem("w_hi_done")
        self.rest_done = s.sem("w_rest_done")
        self.used = s.sem("w_used")

    def load(self, e, i, per, u, src):
        e.wait_ge(self.rest_done, i * per + (u + 1))
        s = u % RING
        e.dma_start(self.raw[:, s, 0:src.shape[1], :], src).then_inc(self.landed[s], 16)

    def split_hi(self, e, i, per, u, nk=UNIT):
        s = u % RING
        e.wait_ge(self.landed[s], i * (16 * (per // RING)) + 16 * (u // RING + 1))
        e.wait_ge(self.used, i * per + (u + 1))
        e.activation(self.hi[:, s, 0:nk, :], self.raw[:, s, 0:nk, :], ACT.Copy).then_inc(self.hi_done, 1)

    def split_rest(self, e, i, per, u, nk=UNIT):
        s = u % RING
        e.wait_ge(self.hi_done, i * per + (u + 1))
        e.tensor_tensor(self.rest[:, s, 0:nk, :], self.raw[:, s, 0:nk, :],
                        self.hi[:, s, 0:nk, :].bitcast(F32), ALU.subtract).then_inc(self.rest_done, 1)

    def multiply(self, e, i, per, u, acc, act, kt0, first, last, nk=UNIT):
        s = u % RING
        e.wait_ge(self.rest_done, i * per + (RING + u + 1))
        for k in range(nk):
            for w, a in ((self.hi, 0), (self.hi, 1), (self.rest, 0)):
                for h in range(2):
                    mm = e.matmul(acc[:, h, 0:HALF], w[:, s, k, :], act[:, kt0 + k, a, h * HALF:(h + 1) * HALF],
                                  start=first and k == 0 and w is self.hi and a == 0,
                                  stop=last and k == nk - 1 and w is self.rest)
        mm.then_inc(self.used, 1)

    def wait_used(self, e, i, per, units):
        e.wait_ge(self.used, i * per + (RING + units))

    def credit_rest(self, e):
        e.sem_inc(self.rest_done, RING)

    def credit_used(self, e):
        e.sem_inc(self.used, RING)


def columns(w, c, kt0, nk=UNIT):
    return w.rearrange("(k p) c -> p k c", p=P)[:, kt0:kt0 + nk, ds(c, P)]


class Norm:
    def __init__(self, s, x, gain_dram, out, const):
        self.x, self.gain_dram, self.out, self.c = x, gain_dram, out, const
        self.sq = s.sb("sq", [P, 2, TOK])
        self.gain = s.sb("gain", [P, KT])
        self.deviation = s.sb("deviation", [P, TOK])
        self.rstd = s.sb("rstd", [P, TOK])
        self.scaled = s.sb("scaled", [P, 2, TOK])
        self.total = s.ps("total", [P, 2, 512])
        self.gain_in = s.sem("gain_in")
        self.sq_ready = s.sem("sq_ready")
        self.sq_used = s.sem("sq_used")
        self.dev_ready = s.sem("dev_ready")
        self.rstd_ready = s.sem("rstd_ready")
        self.scaled_ready = s.sem("scaled_ready")
        self.hi_ready = s.sem("n_hi_ready")
        self.scaled_free = s.sem("scaled_free")

    def load(self, e):
        e.dma_start(self.gain[:], self.gain_dram.rearrange("(k p) -> p k", p=P),
                    allow_slow_non_contiguous=True).then_inc(self.gain_in, 16)

    def scalar(self, e):
        for k in range(KT):
            if k >= 2:
                e.wait_ge(self.sq_used, k - 1)
            e.activation(self.sq[:, k % 2, :], self.x[:, k, :], ACT.Square).then_inc(self.sq_ready, 1)
        e.wait_ge(self.sq_used, KT)
        e.activation(halves(self.deviation[:]), self.total[:, :, 0:HALF], ACT.Sqrt, scale=1.0 / D_MODEL,
                     bias=self.c("eps")).then_inc(self.dev_ready, 1)
        with e.Fori(0, KT // 2) as i:
            for j in range(2):
                e.wait_ge(self.scaled_ready, i * 2 + (j + 1))
                e.activation(self.out[:, ds(i * 2 + j, 1), 0, :], self.scaled[:, j:j + 1, :],
                             ACT.Copy).then_inc(self.hi_ready, 1)

    def tensor(self, e):
        for k in range(KT):
            e.wait_ge(self.sq_ready, k + 1)
            for h in range(2):
                mm = e.matmul(self.total[:, h, 0:HALF], self.c("ones"), self.sq[:, k % 2, h * HALF:(h + 1) * HALF],
                              start=k == 0, stop=k == KT - 1)
            mm.then_inc(self.sq_used, 1)

    def vector(self, e):
        e.wait_ge(self.dev_ready, 1)
        e.reciprocal(self.rstd[:], self.deviation[:]).then_inc(self.rstd_ready, 1)
        e.wait_ge(self.rstd_ready, 1)
        e.wait_ge(self.gain_in, 16)
        e.sem_inc(self.scaled_free, 2)
        with e.Fori(0, KT // 2) as i:
            for j in range(2):
                e.wait_ge(self.scaled_free, i * 2 + (j + 1))
                e.scalar_tensor_tensor(out=self.scaled[:, j:j + 1, :], in0=self.x[:, ds(i * 2 + j, 1), :],
                                       scalar=self.gain[:, ds(i * 2 + j, 1)], in1=self.rstd[:].unsqueeze(1),
                                       op0=ALU.mult, op1=ALU.mult).then_inc(self.scaled_ready, 1)
            for j in range(2):
                e.wait_ge(self.hi_ready, i * 2 + (j + 1))
                e.tensor_tensor(self.out[:, ds(i * 2 + j, 1), 1, :], self.scaled[:, j:j + 1, :],
                                self.out[:, ds(i * 2 + j, 1), 0, :].bitcast(F32),
                                ALU.subtract).then_inc(self.scaled_free, 1)


def stage_prepare(k):
    nc = k.nc
    with Space(nc, "prep") as s:
        rows = s.sb("rows", [P, TB, D_MODEL])
        xT = s.sb("xT", [P, KT, TOK])
        pt = s.ps("pt", [P, 2, 4, P])
        x_in = s.sems("x_in", TB)
        turned_sem = s.sem("turned")
        stored = s.sem("stored")
        evac = s.sem("evac")
        x_out = s.sem("x_out")
        norm = Norm(s, xT, k.g_mix[0], k.act, k.c)
        c_in = s.sem("c_in")
        block = s.block()
        NG = TB * (KT // 4)

        @block.sync
        def _(e):
            e.dma_start(k.const[:], k.const_dram).then_inc(c_in, 16)
            for b in range(4):
                e.dma_start(rows[:, b, :], k.x_prompt[0, b * P:(b + 1) * P, :]).then_inc(x_in[b], 16)
            e.dma_start(rows[0:NS, 4, :], k.x_sample.rearrange("b t d -> (b t) d")).then_inc(x_in[4], 16)
            norm.load(e)
            e.wait_ge(evac, NG)
            e.dma_start(k.xT_dram, xT[:]).then_inc(x_out, 16)
            e.wait_ge(x_out, 16)

        @block.tensor
        def _(e):
            e.wait_ge(c_in, 16)
            n = 0
            for b in range(TB):
                e.wait_ge(x_in[b], 16)
                r = P if b < 4 else NS
                for kg in range(KT // 4):
                    if n >= 2:
                        e.wait_ge(evac, n - 1)
                    for j in range(4):
                        kt = kg * 4 + j
                        mm = e.transpose(pt[:, n % 2, j, 0:r], rows[0:r, b, kt * P:(kt + 1) * P],
                                         k.c("ident")[0:r, 0:r])
                    mm.then_inc(turned_sem, 1)
                    n += 1
            norm.tensor(e)

        @block.vector
        def _(e):
            n = 0
            for b in range(TB):
                r = P if b < 4 else NS
                for kg in range(KT // 4):
                    e.wait_ge(turned_sem, n + 1)
                    e.tensor_copy(xT[:, kg * 4:kg * 4 + 4, b * P:b * P + r], pt[:, n % 2, :, 0:r]).then_inc(evac, 1)
                    n += 1
            norm.vector(e)

        @block.scalar
        def _(e):
            e.wait_ge(evac, NG)
            e.wait_ge(c_in, 16)
            norm.scalar(e)


def stage_ssm_input(k):
    nc = k.nc
    with Space(nc, "ssmin") as s:
        w = Stream(s)
        acc = [s.ps(f"acc{a}", [P, 2, 512]) for a in range(2)]
        acc_free = s.sem("acc_free")
        par_rows = s.sb("par_rows", [ST, 3, P])
        logdt = s.sb("logdt", [ST, 2])
        b_nat = s.sb("b_nat", [P, 2, ST, GC])
        c_nat = s.sb("c_nat", [P, 2, CT, 2, GS])
        par = s.sb("par", [P, 3, ST])
        t = s.sb("t", [P, 16, ST])
        bb = s.sb("bb", [P, 2, ST, 2 * GC])
        tmp = s.sb("tmp", [P, ST, GC])
        pw = s.sb("pw", [P, 4, ST])
        tw = s.sb("tw", [P, 2, ST, LO // 2])
        pp = s.ps("pp", [P, 2, 512])
        par_in, dt_done, rows_done = s.sem("par_in"), s.sem("dt_done"), s.sem("rows_done")
        bc_in = s.sem("bc_in")
        par_turned, par_ready = s.sem("par_turned"), s.sem("par_ready")
        act_done, angles_ready, turn_ready = s.sem("act_done"), s.sem("angles_ready"), s.sem("turn_ready")
        bb_done, bb_turned, bb_free = s.sem("bb_done"), s.sem("bb_turned"), s.sem("bb_free")
        chain_sem, pool_chain = s.sem("chain"), s.sem("pool_chain")
        block = s.block()
        U = D_MODEL // P // UNIT
        PER = U * 2
        V_END = 3 * NH * DV

        @block.sync
        def _(e):
            for n, src in enumerate((k.ssm_a_re[0], k.ssm_a_im[0])):
                e.dma_start(par_rows[:, n, :], src.rearrange("(t g) p -> t (g p)", g=2)).then_inc(par_in, 16)
            e.dma_start(logdt[:], k.ssm_log_dt[0].rearrange("(t g) -> t g", g=2)).then_inc(par_in, 16)
            e.dma_start(k.ssm_d_col[:], k.ssm_d[0].rearrange("(t g) c -> (g c) t", t=CT),
                        allow_slow_non_contiguous=True).then_inc(par_in, 16)
            with e.Fori(0, CT // 2) as i:
                for u in range(PER):
                    w.load(e, i, PER, u, columns(k.w_in[0], i * (2 * P) + (V_END + P * (u // U)), UNIT * (u % U)))

        @block.gpsimd
        def _(e):
            for n, src in enumerate((k.ssm_b_re[0], k.ssm_b_im[0])):
                e.dma_start(b_nat[:, n, :, :], src.rearrange("(t g) p c -> (g p) t c", g=2)).then_inc(bc_in, 16)
            for n, src in enumerate((k.ssm_c_re[0], k.ssm_c_im[0])):
                for r in range(2):
                    e.dma_start(c_nat[:, n, :, r, :],
                                src.rearrange("(t g) c p -> (g c) t p", t=CT)).then_inc(bc_in, 16)
            ch = Chain(e, pool_chain)
            e.wait_ge(turn_ready, 1)
            ch.step(e.memset(k.tw_lo[:, 0, :, 0:1], 1.0))
            ch.step(e.memset(k.tw_lo[:, 1, :, 0:1], 0.0))
            ch.step(e.memset(k.tw_hi[:, 0, :, 0:1], 1.0))
            ch.step(e.memset(k.tw_hi[:, 1, :, 0:1], 0.0))
            for table, size in ((k.tw_lo, LO), (k.tw_hi, HI)):
                n = 1
                while n < size:
                    re, im = table[:, 0, :, 0:n], table[:, 1, :, 0:n]
                    pr, pi = wide(pw[:, 0, :], n), wide(pw[:, 1, :], n)
                    ta, tb_ = tw[:, 0, :, 0:n], tw[:, 1, :, 0:n]
                    ch.did(e.tensor_tensor(ta, re, pr, ALU.mult))
                    ch.step(e.tensor_tensor(tb_, im, pi, ALU.mult))
                    ch.step(e.tensor_tensor(table[:, 0, :, n:2 * n], ta, tb_, ALU.subtract))
                    ch.did(e.tensor_tensor(ta, re, pi, ALU.mult))
                    ch.step(e.tensor_tensor(tb_, im, pr, ALU.mult))
                    ch.step(e.tensor_tensor(table[:, 1, :, n:2 * n], ta, tb_, ALU.add))
                    ch.did(e.tensor_tensor(pw[:, 2, :], pw[:, 0, :], pw[:, 0, :], ALU.mult))
                    ch.step(e.tensor_tensor(pw[:, 3, :], pw[:, 1, :], pw[:, 1, :], ALU.mult))
                    ch.did(e.tensor_tensor(tw[:, 0, :, 0], pw[:, 0, :], pw[:, 1, :], ALU.mult))
                    ch.wait()
                    ch.step(e.tensor_tensor(pw[:, 0, :], pw[:, 2, :], pw[:, 3, :], ALU.subtract))
                    ch.step(e.tensor_tensor(pw[:, 1, :], tw[:, 0, :, 0], tw[:, 0, :, 0], ALU.add))
                    n *= 2

        @block.scalar
        def _(e):
            e.sem_inc(acc_free, 2)
            e.wait_ge(par_in, 64)
            e.activation(logdt[:], logdt[:], ACT.Exp).then_inc(dt_done, 1)
            e.wait_ge(angles_ready, 1)
            e.activation(t[:, 3, :], t[:, 0, :], ACT.Exp).then_inc(act_done, 1)
            e.activation(t[:, 4, :], t[:, 1, :], ACT.Sin).then_inc(act_done, 1)
            e.activation(t[:, 5, :], t[:, 2, :], ACT.Sin).then_inc(act_done, 1)
            with e.Fori(0, CT // 2) as i:
                for a in range(2):
                    for u in range(U):
                        w.split_hi(e, i, PER, a * U + u)
                for a in range(2):
                    w.wait_used(e, i, PER, (a + 1) * U)
                    e.activation(k.uT[:, ds(i * 2 + a, 1), :].rearrange("p o (a n) -> p (o a) n", a=2),
                                 acc[a][:, :, 0:HALF], ACT.Copy).then_inc(acc_free, 1)

        @block.vector
        def _(e):
            ch = Chain(e, chain_sem)
            w.credit_rest(e)
            e.wait_ge(dt_done, 1)
            e.tensor_copy(par_rows[:, 2, :].rearrange("p (g q) -> p g q", g=2), wide(logdt[:], GS)).then_inc(rows_done, 1)
            e.wait_ge(par_turned, 3)
            e.tensor_copy(par[:], pp[:, 0, 0:3 * ST].rearrange("p (n t) -> p n t", n=3)).then_inc(par_ready, 1)
            e.wait_ge(par_ready, 1)
            are, aim, dt = par[:, 0, :], par[:, 1, :], par[:, 2, :]
            T = lambda n: t[:, n, :]
            ch.did(e.tensor_tensor(T(0), are, dt, ALU.mult))
            ch.step(e.tensor_tensor(T(1), aim, dt, ALU.mult))
            ch.step(e.tensor_scalar(T(6), T(1), 1.0 / (2 * PI), ROUND, ALU.mult, ALU.add))
            ch.step(e.tensor_scalar(T(6), T(6), ROUND, None, ALU.subtract))
            ch.step(e.tensor_scalar(T(7), T(6), -TWO_PI_A, None, ALU.mult))
            ch.step(e.tensor_tensor(T(1), T(1), T(7), ALU.add))
            ch.step(e.tensor_scalar(T(7), T(6), -TWO_PI_B, None, ALU.mult))
            ch.step(e.tensor_tensor(T(1), T(1), T(7), ALU.add))
            ch.step(e.tensor_scalar(T(1), T(1), 3.1415925, -3.1415925, ALU.min, ALU.max))
            ch.step(e.tensor_scalar(T(2), T(1), PI / 2, None, ALU.add))
            ch.step(e.tensor_scalar(T(7), T(2), PI, -2 * PI, ALU.is_gt, ALU.mult))
            ch.step(e.tensor_tensor(T(2), T(2), T(7), ALU.add))
            ch.step(e.tensor_scalar(T(2), T(2), 3.1415925, -3.1415925, ALU.min, ALU.max))
            e.tensor_copy(T(15), T(2)).then_inc(angles_ready, 1)
            e.wait_ge(act_done, 3)
            mag, sin, cos = T(3), T(4), T(5)
            ch.did(e.tensor_copy(pw[:, 0, :], cos))
            e.tensor_copy(pw[:, 1, :], sin).then_inc(turn_ready, 1)
            ch.did(e.tensor_copy(k.mag[:], mag))
            ch.did(e.tensor_tensor(k.ab[:, 0, :], mag, cos, ALU.mult))
            ch.step(e.tensor_tensor(k.ab[:, 1, :], mag, sin, ALU.mult))
            ch.did(e.tensor_tensor(T(8), are, are, ALU.mult))
            ch.step(e.tensor_tensor(T(9), aim, aim, ALU.mult))
            ch.step(e.tensor_tensor(T(8), T(8), T(9), ALU.add))
            ch.step(e.reciprocal(T(8), T(8)))
            ch.step(e.tensor_scalar(T(9), k.ab[:, 0, :], -1.0, None, ALU.add))
            ch.did(e.tensor_tensor(T(10), T(9), are, ALU.mult))
            ch.step(e.tensor_tensor(T(11), k.ab[:, 1, :], aim, ALU.mult))
            ch.step(e.tensor_tensor(T(10), T(10), T(11), ALU.add))
            ch.step(e.tensor_tensor(T(10), T(10), T(8), ALU.mult))
            ch.did(e.tensor_tensor(T(11), k.ab[:, 1, :], are, ALU.mult))
            ch.step(e.tensor_tensor(T(12), T(9), aim, ALU.mult))
            ch.step(e.tensor_tensor(T(11), T(11), T(12), ALU.subtract))
            ch.step(e.tensor_tensor(T(11), T(11), T(8), ALU.mult))
            e.wait_ge(bc_in, 6 * 16)
            ch.step(e.memset(bb[:], 0.0))
            for out, x0, x1, op in ((0, 0, 1, ALU.subtract), (1, 1, 0, ALU.add)):
                ch.step(e.tensor_tensor(tmp[:], b_nat[:, x1, :, :], wide(T(11), GC), ALU.mult))
                for g in range(2):
                    r = slice(g * GS, (g + 1) * GS)
                    o = bb[r, out, :, g * GC:(g + 1) * GC]
                    ch.step(e.tensor_tensor(o, b_nat[r, x0, :, :], wide(T(10)[r, :], GC), ALU.mult))
                    ch.step(e.tensor_tensor(o, o, tmp[r, :, :], op))
            ch.did(e.memset(k.CTm[:], 0.0))
            ch.wait()
            e.tensor_copy(T(14), T(11)).then_inc(bb_done, 1)
            n = 0
            for m in range(2):
                for T8 in range(CT):
                    e.wait_ge(bb_turned, n + 1)
                    e.tensor_copy(k.BT[:, m, T8, :], pp[:, n % 2, 0:P]).then_inc(bb_free, 1)
                    n += 1
            for m in range(2):
                for T8 in range(CT):
                    e.wait_ge(bb_turned, n + 1)
                    src = pp[:, n % 2, 0:P].rearrange("p (q g c) -> p q g c", q=4, g=2)
                    for g in range(2):
                        r = slice(g * GS, (g + 1) * GS)
                        ins = e.tensor_scalar(k.CTm[r, m, T8 * 4:T8 * 4 + 4, g * GC:(g + 1) * GC], src[r, :, g, :],
                                              1.0 if m == 0 else -1.0, None, ALU.mult)
                    ins.then_inc(bb_free, 1)
                    n += 1
            with e.Fori(0, CT // 2) as i:
                for u in range(PER):
                    w.split_rest(e, i, PER, u)

        @block.tensor
        def _(e):
            w.credit_used(e)
            e.wait_ge(par_in, 64)
            e.wait_ge(rows_done, 1)
            for n in range(3):
                e.transpose(pp[:, 0, n * ST:(n + 1) * ST], par_rows[:, n, :],
                            k.c("ident")[0:ST, 0:ST]).then_inc(par_turned, 1)
            e.wait_ge(bb_done, 1)
            n = 0
            for m in range(2):
                for T8 in range(CT):
                    if n >= 2:
                        e.wait_ge(bb_free, n - 1)
                    e.transpose(pp[:, n % 2, 0:P], bb[:, m, T8 * 4:T8 * 4 + 4, :].rearrange("p t c -> p (t c)"),
                                k.c("ident")).then_inc(bb_turned, 1)
                    n += 1
            for m in range(2):
                for T8 in range(CT):
                    e.wait_ge(bb_free, n - 1)
                    e.transpose(pp[:, n % 2, 0:P], c_nat[:, m, T8, :, :].rearrange("p r q -> p (r q)"),
                                k.c("ident")).then_inc(bb_turned, 1)
                    n += 1
            with e.Fori(0, CT // 2) as i:
                for a in range(2):
                    e.wait_ge(acc_free, i * 2 + (a + 1))
                    for u in range(U):
                        w.multiply(e, i, PER, a * U + u, acc[a], k.act, u * UNIT, u == 0, u == U - 1)


def stage_scan(k):
    nc = k.nc
    with Space(nc, "scan") as s:
        w = Stream(s)
        acc = [s.ps(f"acc{a}", [P, 2, 512]) for a in range(2)]
        bu = s.ps("bu", [P, 2, 512])
        y = s.ps("y", [P, 512])
        b_stage = [s.sb(f"b_stage{q}", [P, 2, P]) for q in range(4)]
        c_stage = [s.sb(f"c_stage{q}", [P, 2, P]) for q in range(4)]
        d_stage = s.sb("d_stage", [P, P])
        tw = s.sb("tw", [P, 2, 2, NP])
        tw_tmp = s.sb("tw_tmp", [P, 2, NP])
        v = s.sb("v", [P, 2, NP])
        m = s.sb("m", [P, 2, NP])
        h = s.sb("h", [P, 2, 2, NP])
        zout = s.sb("zout", [P, 2, TOK])
        yout = s.sb("yout", [P, NP])
        acc_free, evac = s.sem("acc_free"), s.sem("evac")
        z_stored = s.sems("z_stored", 2)
        zero_done, staged, d_staged = s.sem("zero_done"), s.sem("staged"), s.sem("d_staged")
        bu_ready, bu_free = s.sem("bu_ready"), s.sem("bu_free")
        tw_ready, tw_free = s.sem("tw_ready"), s.sem("tw_free")
        h_ready, y_done, y_whole, y_free = s.sem("h_ready"), s.sem("y_done"), s.sem("y_whole"), s.sem("y_free")
        y_out, y_stored = s.sem("y_out"), s.sem("y_stored")
        vec_chain, pool_chain = s.sem("vec_chain"), s.sem("pool_chain")
        block = s.block()
        U = KT // UNIT
        PER1, PER2 = 4 * U, 2 * U
        N1, N2 = CT, 12
        BASE2 = N1 * PER1
        U_END = 3 * NH * DV + CT * P

        def column1(i, q):
            return i * (3 * P) + q * P if q < 3 else i * P + U_END

        def z_row(i, a, second):
            if second:
                return i * 2 + (24 + CT + a)
            return i * 3 + a if a < 3 else i + 24

        @block.sync
        def _(e):
            with e.Fori(0, N1) as i:
                for u in range(PER1):
                    w.load(e, i, PER1, u, columns(k.w_in[0], column1(i, u // U), UNIT * (u % U)))
            with e.Fori(0, N2) as i:
                for u in range(PER2):
                    w.load(e, i, PER2, BASE2 + u,
                           columns(k.w_in[0], i * (2 * P) + (U_END + CT * P + P * (u // U)), UNIT * (u % U)))

        @block.gpsimd
        def _(e):
            w.credit_rest(e)
            for q in range(4):
                e.memset(b_stage[q][:], 0.0).then_inc(zero_done, 1)
                e.memset(c_stage[q][:], 0.0).then_inc(zero_done, 1)
            ch = Chain(e, pool_chain)
            with e.Fori(0, N1) as i:
                ch.begin(i, 16)
                for q in range(4):
                    w.split_rest(e, i, PER1, q * U)
                    n = i * 4 + q
                    hi = [k.tw_hi[:, c, ds(n, 1), :].rearrange("p o n -> p (o n)") for c in range(2)]
                    lo = [k.tw_lo[:, c, ds(n, 1), :].rearrange("p o n -> p (o n)") for c in range(2)]
                    both = lambda a, b: (wide(hi[a], LO), turned(lo[b], HI))
                    grid = lambda t: t.rearrange("p (a b) -> p a b", a=HI)
                    e.wait_ge(tw_free, n + 1)
                    e.nop(nofuse=True)
                    ch.did(e.tensor_tensor(grid(tw_tmp[:, 0, :]), *both(0, 0), ALU.mult))
                    ch.step(e.tensor_tensor(grid(tw_tmp[:, 1, :]), *both(1, 1), ALU.mult))
                    w.split_rest(e, i, PER1, q * U + 1)
                    e.tensor_tensor(tw[:, q % 2, 0, :], tw_tmp[:, 0, :], tw_tmp[:, 1, :],
                                    ALU.subtract).then_inc(tw_ready, 1)
                    e.wait_ge(tw_ready, n * 2 + 1)
                    e.nop(nofuse=True)
                    ch.did(e.tensor_tensor(grid(tw_tmp[:, 0, :]), *both(0, 1), ALU.mult))
                    ch.step(e.tensor_tensor(grid(tw_tmp[:, 1, :]), *both(1, 0), ALU.mult))
                    w.split_rest(e, i, PER1, q * U + 2)
                    e.tensor_tensor(tw[:, q % 2, 1, :], tw_tmp[:, 0, :], tw_tmp[:, 1, :],
                                    ALU.add).then_inc(tw_ready, 1)
                    e.wait_ge(tw_ready, n * 2 + 2)
                    w.split_rest(e, i, PER1, q * U + 3)
            ch.end(N1)
            with e.Fori(0, N2) as i:
                for u in range(PER2):
                    w.split_rest(e, i, PER2, BASE2 + u)

        @block.vector
        def _(e):
            ch = Chain(e, vec_chain)
            e.sem_inc(tw_free, 2)
            e.sem_inc(bu_free, 1)
            with e.Fori(0, N1) as i:
                ch.begin(i, 4 * 14)
                for q in range(4):
                    n = i * 4 + q
                    re, im = tw[:, q % 2, 0, :], tw[:, q % 2, 1, :]
                    e.wait_ge(bu_ready, n + 1)
                    e.wait_ge(tw_ready, n * 2 + 2)
                    ch.did(e.tensor_tensor(m[:, 0, :], bu[:, 0, :], re, ALU.mult))
                    ch.step(e.tensor_tensor(m[:, 1, :], bu[:, 1, :], im, ALU.mult))
                    ch.step(e.tensor_tensor(v[:, 0, :], m[:, 0, :], m[:, 1, :], ALU.add))
                    ch.did(e.tensor_tensor(m[:, 0, :], bu[:, 1, :], re, ALU.mult))
                    ch.step(e.tensor_tensor(m[:, 1, :], bu[:, 0, :], im, ALU.mult))
                    e.sem_inc(bu_free, 1)
                    ch.step(e.tensor_tensor(v[:, 1, :], m[:, 0, :], m[:, 1, :], ALU.subtract))
                    decay = k.mag[:, ds(n, 1)].broadcast_to([P, NP])
                    ch.did(e.tensor_tensor_scan(m[:, 0, :], decay, v[:, 0, :], 0.0, ALU.mult, ALU.add))
                    ch.step(e.tensor_tensor_scan(m[:, 1, :], decay, v[:, 1, :], 0.0, ALU.mult, ALU.add))
                    hr, hi_ = h[:, q % 2, 0, :], h[:, q % 2, 1, :]
                    e.wait_ge(y_done, n + 3)
                    ch.did(e.tensor_tensor(hr, m[:, 0, :], re, ALU.mult))
                    ch.did(e.tensor_tensor(v[:, 0, :], m[:, 1, :], im, ALU.mult))
                    ch.did(e.tensor_tensor(hi_, m[:, 0, :], im, ALU.mult))
                    ch.step(e.tensor_tensor(v[:, 1, :], m[:, 1, :], re, ALU.mult))
                    e.tensor_tensor(hr, hr, v[:, 0, :], ALU.subtract).then_inc(h_ready, 1)
                    e.tensor_tensor(hi_, hi_, v[:, 1, :], ALU.add).then_inc(h_ready, 1)
                    e.wait_ge(h_ready, n * 2 + 2)
                    e.sem_inc(tw_free, 1)
                    ch.did(e.tensor_copy(k.fin[:, 0, ds(n, 1)], hr[:, NP - 1:NP]))
                    ch.step(e.tensor_copy(k.fin[:, 1, ds(n, 1)], hi_[:, NP - 1:NP]))
            ch.end(N1)

        @block.scalar
        def _(e):
            e.sem_inc(acc_free, 2)
            e.sem_inc(z_stored[0], 16)
            e.sem_inc(z_stored[1], 16)
            e.sem_inc(y_stored, 16)
            e.sem_inc(y_free, 1)
            e.wait_ge(zero_done, 8)

            def evacuate(i, t, second, sigmoid):
                a = t % 2
                w.wait_used(e, i, PER2 if second else PER1, (BASE2 if second else 0) + (t + 1) * U)
                uses = (N1 * 2 if second else 0) + t // 2
                step = 1 if second else 2
                e.wait_ge(z_stored[a], i * (16 * step) + 16 * (uses + 1))
                e.activation(halves(zout[:, a, :]), acc[a][:, :, 0:HALF],
                             ACT.Sigmoid if sigmoid else ACT.Copy).then_inc(evac, 1)
                e.wait_ge(evac, i * (2 * step) + ((N1 * 4 if second else 0) + t + 1))
                e.sem_inc(acc_free, 1)
                e.dma_start(k.z_dram[ds(z_row(i, t, second), 1)].rearrange("o p n -> p (o n)"),
                            zout[:, a, :]).then_inc(z_stored[a], 16)

            def body1(i, first):
                for q in range(4):
                    e.wait_ge(y_done, i * 4 + (q + 1))
                    r = slice(32 * q, 32 * q + 32)
                    e.activation(b_stage[q][r, :, :], k.BT[r, :, ds(i, 1), :].rearrange("p m o n -> p (m o) n"),
                                 ACT.Copy).then_inc(staged, 1)
                    e.activation(c_stage[q][:, :, r], k.CTm[:, :, ds(i * 4 + q, 1), :].rearrange("p m o n -> p (m o) n"),
                                 ACT.Copy).then_inc(staged, 1)
                    if q == 3:
                        e.activation(d_stage[:], k.c("ident"), ACT.Copy,
                                     scale=k.ssm_d_col[:, ds(i, 1)]).then_inc(d_staged, 1)
                    for u in range(U):
                        w.split_hi(e, i, PER1, q * U + u)
                    if q:
                        evacuate(i, q - 1, False, False)
                    elif not first:
                        evacuate(i - 1, 3, False, True)
                        finish_y(i - 1)

            def finish_y(i):
                e.wait_ge(y_whole, i + 1)
                e.wait_ge(y_stored, i * 16 + 16)
                e.activation(yout[:], y[:], ACT.Gelu_apprx_tanh).then_inc(y_out, 1)
                e.wait_ge(y_out, i + 1)
                e.sem_inc(y_free, 1)
                e.dma_start(k.y_dram[ds(i, 1), :, 0:NP].rearrange("o p n -> p (o n)"), yout[:]).then_inc(y_stored, 16)

            def body2(i, first):
                for t in range(2):
                    for u in range(U):
                        w.split_hi(e, i, PER2, BASE2 + t * U + u)
                    if t == 1:
                        evacuate(i, 0, True, True)
                    elif not first:
                        evacuate(i - 1, 1, True, True)

            body1(0, True)
            with e.Fori(1, N1) as i:
                body1(i, False)
            for u in range(U):
                w.split_hi(e, 0, PER2, BASE2 + u)
            evacuate(N1 - 1, 3, False, True)
            finish_y(N1 - 1)
            for u in range(U, 2 * U):
                w.split_hi(e, 0, PER2, BASE2 + u)
            evacuate(0, 0, True, True)
            with e.Fori(1, N2) as i:
                body2(i, False)
            evacuate(N2 - 1, 1, True, True)
            for a in range(2):
                e.wait_ge(z_stored[a], 16 * (2 * N1 + N2 + 1))
            e.wait_ge(y_stored, 16 * (N1 + 1))

        @block.tensor
        def _(e):
            w.credit_used(e)
            e.sem_inc(y_done, 4)
            with e.Fori(0, N1) as i:
                for q in range(4):
                    n = i * 4 + q
                    e.wait_ge(staged, i * 8 + (2 * q + 2))
                    e.wait_ge(bu_free, n + 1)
                    for c in range(2):
                        mm = e.matmul(bu[:, c, :], b_stage[q][:, c, :],
                                      k.uT[:, ds(i, 1), 0:NP].rearrange("p o n -> p (o n)"), start=True, stop=True)
                    mm.then_inc(bu_ready, 1)
                    e.wait_ge(acc_free, n + 1)
                    for u in range(U):
                        w.multiply(e, i, PER1, q * U + u, acc[q % 2], k.act, u * UNIT, u == 0, u == U - 1)
                    if q == 0:
                        e.wait_ge(y_free, i + 1)
                    e.wait_ge(h_ready, n * 2 + 2)
                    for c in range(2):
                        mm = e.matmul(y[:], c_stage[q][:, c, :], h[:, q % 2, c, :], start=q == 0 and c == 0, stop=False)
                    mm.then_inc(y_done, 1)
                e.wait_ge(d_staged, i + 1)
                e.matmul(y[:], d_stage[:], k.uT[:, ds(i, 1), 0:NP].rearrange("p o n -> p (o n)"),
                         start=False, stop=True).then_inc(y_whole, 1)
            with e.Fori(0, N2) as i:
                for t in range(2):
                    e.wait_ge(acc_free, i * 2 + (N1 * 4 + t + 1))
                    for u in range(U):
                        w.multiply(e, i, PER2, BASE2 + t * U + u, acc[t], k.act, u * UNIT, u == 0, u == U - 1)


def stage_scan_sample(k):
    nc = k.nc
    with Space(nc, "samp") as s:
        b_stage = s.sb("b_stage", [P, 4, 2, P])
        c_stage = s.sb("c_stage", [P, 4, 2, P])
        d_stage = s.sb("d_stage", [P, P])
        bu_ps = s.ps("bu_ps", [P, 4, 2, NS])
        y_ps = s.ps("y_ps", [P, NS])
        tp = s.ps("tp", [P, 2, 512])
        bu = s.sb("bu", [P, 2, ST, NS])
        H = s.sb("H", [P, 2, ST, NB, NQ])
        rows = s.sb("rows", [P, 2, 2, P])
        h0 = s.sb("h0", [P, 2, ST, NB])
        x = s.sb("x", [P, 3, ST, NB])
        last = s.sb("last", [P, 2, 2, 4, ST])
        out_rows = s.sb("out_rows", [P, 2, 3, P])
        ys = s.sb("ys", [P, CT, NS])
        rows_in, zero_done, staged, bu_ready, bu_free = (s.sem(x_) for x_ in
                                                         ("rows_in", "zero_done", "staged", "bu_ready", "bu_free"))
        turned_sem, turned_free, steps, last_done, out_done, stored = (
            s.sem(x_) for x_ in ("turned", "turned_free", "steps", "last_done", "out_done", "stored"))
        c_staged, y_ready, y_free = s.sem("c_staged"), s.sem("y_ready"), s.sem("y_free")
        chain_sem = s.sem("chain")
        block = s.block()

        @block.sync
        def _(e):
            for c, src in enumerate((k.state_ssm_re[0], k.state_ssm_im[0])):
                for hf in range(2):
                    e.dma_start(rows[:, c, hf, :], src[hf * 4:hf * 4 + 4].rearrange("b (t g) p -> (b t) (g p)", g=2)
                                ).then_inc(rows_in, 16)
            e.wait_ge(out_done, 6)
            for c in range(2):
                e.dma_start(k.new_ssm_prompt[c][0, 0].rearrange("(t g) p -> t (g p)", g=2),
                            out_rows[0:ST, c, 2, :]).then_inc(stored, 16)
                for hf in range(2):
                    e.dma_start(k.new_ssm_sample[c][0, hf * 4:hf * 4 + 4].rearrange("b (t g) p -> (b t) (g p)", g=2),
                                out_rows[:, c, hf, :]).then_inc(stored, 16)
            e.wait_ge(y_free, CT + 1)
            e.dma_start(k.y_dram[:, :, NP:TOK].rearrange("t p n -> p t n"), ys[:]).then_inc(stored, 16)
            e.wait_ge(stored, 16 * 7)

        @block.gpsimd
        def _(e):
            e.memset(b_stage[:], 0.0).then_inc(zero_done, 1)
            e.memset(c_stage[:], 0.0).then_inc(zero_done, 1)

        @block.scalar
        def _(e):
            e.sem_inc(y_free, 1)
            e.wait_ge(zero_done, 2)
            with e.Fori(0, CT) as i:
                e.wait_ge(bu_ready, i + 1)
                for q in range(4):
                    r = slice(32 * q, 32 * q + 32)
                    e.activation(b_stage[r, q, :, :], k.BT[r, :, ds(i, 1), :].rearrange("p m o n -> p (m o) n"),
                                 ACT.Copy).then_inc(staged, 1)
            with e.Fori(0, CT) as i:
                e.wait_ge(y_ready, i + 1)
                for q in range(4):
                    r = slice(32 * q, 32 * q + 32)
                    e.activation(c_stage[:, q, :, r], k.CTm[:, :, ds(i * 4 + q, 1), :].rearrange("p m o n -> p (m o) n"),
                                 ACT.Copy).then_inc(c_staged, 1)
                e.activation(d_stage[:], k.c("ident"), ACT.Copy, scale=k.ssm_d_col[:, ds(i, 1)]).then_inc(c_staged, 1)
                e.wait_ge(y_ready, i + 2)
                e.activation(ys[:, ds(i, 1), :].rearrange("p o n -> p (o n)"), y_ps[:],
                             ACT.Gelu_apprx_tanh).then_inc(y_free, 1)

        @block.tensor
        def _(e):
            e.sem_inc(bu_ready, 1)
            e.sem_inc(y_ready, 1)
            with e.Fori(0, CT) as i:
                e.wait_ge(staged, i * 4 + 4)
                e.wait_ge(bu_free, i + 1)
                for q in range(4):
                    for c in range(2):
                        mm = e.matmul(bu_ps[:, q, c, :], b_stage[:, q, c, :],
                                      k.uT[:, ds(i, 1), NP:TOK].rearrange("p o n -> p (o n)"), start=True, stop=True)
                mm.then_inc(bu_ready, 1)
            e.wait_ge(rows_in, 64)
            n = 0
            for c in range(2):
                for hf in range(2):
                    if n >= 2:
                        e.wait_ge(turned_free, n - 1)
                    e.transpose(tp[:, n % 2, 0:P], rows[:, c, hf, :], k.c("ident")).then_inc(turned_sem, 1)
                    n += 1
            e.wait_ge(last_done, 1)
            for c in range(2):
                for hf in range(3):
                    e.wait_ge(turned_free, n - 1)
                    if hf < 2:
                        e.transpose(tp[:, n % 2, 0:P], last[:, c, hf, :, :].rearrange("p b t -> p (b t)"),
                                    k.c("ident")).then_inc(turned_sem, 1)
                    else:
                        e.transpose(tp[0:ST, n % 2, 0:P], k.fin[:, c, :], k.c("ident")).then_inc(turned_sem, 1)
                    n += 1
            with e.Fori(0, CT) as i:
                e.wait_ge(c_staged, i * 5 + 5)
                e.wait_ge(y_free, i + 1)
                for q in range(4):
                    for c in range(2):
                        e.matmul(y_ps[:], c_stage[:, q, c, :],
                                 H[:, c, ds(i * 4 + q, 1), :, :].rearrange("p o b t -> p (o b t)"),
                                 start=q == 0 and c == 0, stop=False)
                e.matmul(y_ps[:], d_stage[:], k.uT[:, ds(i, 1), NP:TOK].rearrange("p o n -> p (o n)"),
                         start=False, stop=True).then_inc(y_ready, 1)

        @block.vector
        def _(e):
            ch = Chain(e, chain_sem)
            e.sem_inc(bu_free, 1)
            with e.Fori(0, CT) as i:
                e.wait_ge(bu_ready, i + 2)
                e.tensor_copy(bu[:, :, ds(i * 4, 4), :].rearrange("p c q n -> p q c n"), bu_ps[:]).then_inc(bu_free, 1)
            n = 0
            for c in range(2):
                for hf in range(2):
                    e.wait_ge(turned_sem, n + 1)
                    e.tensor_copy(h0[:, c, :, hf * 4:hf * 4 + 4].rearrange("p t b -> p b t"),
                                  tp[:, n % 2, 0:P].rearrange("p (b t) -> p b t", b=4)).then_inc(turned_free, 1)
                    n += 1
            e.wait_ge(turned_free, 4)
            e.wait_ge(bu_free, CT + 1)
            ar, ai = wide(k.ab[:, 0, :], NB), wide(k.ab[:, 1, :], NB)
            x0, x1, x2 = (x[:, j, :, :] for j in range(3))
            for t in range(NQ):
                pr, pi = (h0[:, c, :, :] if t == 0 else H[:, c, :, :, t - 1] for c in range(2))
                br, bi = (bu[:, c, :, :].rearrange("p s (b t) -> p s b t", b=NB)[:, :, :, t] for c in range(2))
                hr, hi_ = H[:, 0, :, :, t], H[:, 1, :, :, t]
                ch.did(e.tensor_tensor(x0, pr, ar, ALU.mult))
                ch.step(e.tensor_tensor(x1, pi, ai, ALU.mult))
                ch.step(e.tensor_tensor(x0, x0, x1, ALU.subtract))
                ch.step(e.tensor_tensor(hr, x0, br, ALU.add))
                ch.did(e.tensor_tensor(x0, pi, ar, ALU.mult))
                ch.step(e.tensor_tensor(x1, pr, ai, ALU.mult))
                ch.step(e.tensor_tensor(x0, x0, x1, ALU.add))
                ch.step(e.tensor_tensor(hi_, x0, bi, ALU.add))
            for c in range(2):
                for hf in range(2):
                    ch.step(e.tensor_copy(last[:, c, hf, :, :],
                                          H[:, c, :, hf * 4:hf * 4 + 4, NQ - 1].rearrange("p t b -> p b t")))
            e.tensor_copy(x[:, 2, 0, 0:1], last[:, 0, 0, 0, 0:1]).then_inc(last_done, 1)
            for c in range(2):
                for hf in range(3):
                    e.wait_ge(turned_sem, n + 1)
                    r = P if hf < 2 else ST
                    ins = e.tensor_copy(out_rows[0:r, c, hf, :], tp[0:r, n % 2, 0:P])
                    ins.then_inc(turned_free, 1)
                    n += 1
                    e.wait_ge(turned_free, n)
                    e.sem_inc(out_done, 1)


def stage_attention_prompt(k):
    nc = k.nc
    with Space(nc, "att") as s:
        raw = s.sb("raw", [P, 3, TOK])
        sq = s.sb("sq", [P, TOK])
        dev = s.sb("dev", [P, TOK])
        rstd = s.sb("rstd", [P, TOK])
        normed = s.sb("normed", [P, TOK])
        turn = s.sb("turn", [P, TOK])
        qk = s.sb("qk", [P, 2, TOK])
        k_rows = s.sb("k_rows", [P, TB, P])
        v_rows = s.sb("v_rows", [P, TB, P])
        gains = s.sb("gains", [P, 2])
        lam_in = s.sb("lam_in", [DK, 2, 2])
        lam_prod = s.sb("lam_prod", [DK, 2])
        lam_exp = s.sb("lam_exp", [P, 2])
        e_buf = s.sb("e_buf", [P, 2, 2, NP])
        wT = s.sb("wT", [P, 2, 4, P])
        stat = s.sb("stat", [P, 2, 8])
        ss = s.ps("ss", [P, 2, 512])
        tp = s.ps("tp", [P, 2, 512])
        S = s.ps("S", [P, 2, 512])
        tw = s.ps("tw", [P, 4, P])
        o = s.ps("o", [P, NP])
        par_in, lam_a, lam_b, lam_c, zero_lam = (s.sem(x) for x in ("par_in", "lam_a", "lam_b", "lam_c", "zero_lam"))
        raw_in = s.sems("raw_in", 3)
        raw_free = s.sems("raw_free", 3)
        sq_ready, ss_ready, dev_ready, normed_ready, rot_ready, qk_ready = (
            s.sem(x) for x in ("sq_ready", "ss_ready", "dev_ready", "normed_ready", "rot_ready", "qk_ready"))
        tp_ready, tp_free, rows_free = s.sem("tp_ready"), s.sem("tp_free"), s.sem("rows_free")
        rows_stored = s.sems("rows_stored", 2)
        S_ready, S_max, e_ready, w_ready, tw_ready, wT_ready, o_ready, o_free = (
            s.sem(x) for x in ("S_ready", "S_max", "e_ready", "w_ready", "tw_ready", "wT_ready", "o_ready", "o_free"))
        pv_done = s.sem("pv_done")
        chain_sem = s.sem("chain")
        block = s.block()
        SCALE = DK ** -0.5

        @block.sync
        def _(e):
            for m in range(2):
                e.dma_start(gains[m * DK:(m + 1) * DK, 0:1], k.g_q[0, m].rearrange("(p o) -> p o", o=1),
                            allow_slow_non_contiguous=True).then_inc(par_in, 16)
                e.dma_start(gains[m * DK:(m + 1) * DK, 1:2], k.g_k[0, m].rearrange("(p o) -> p o", o=1),
                            allow_slow_non_contiguous=True).then_inc(par_in, 16)
            e.dma_start(lam_in[:, 0, :], k.lambda_q[0].rearrange("m p -> p m"),
                        allow_slow_non_contiguous=True).then_inc(par_in, 16)
            e.dma_start(lam_in[:, 1, :], k.lambda_k[0].rearrange("m p -> p m"),
                        allow_slow_non_contiguous=True).then_inc(par_in, 16)
            for r in range(2):
                e.sem_inc(rows_stored[r], 32)
            with e.Fori(0, NH) as i:
                for j in range(3):
                    e.wait_ge(raw_free[j], i + 1)
                    e.dma_start(raw[:, j, :], k.z_dram[ds(i + 8 * j, 1)].rearrange("o p n -> p (o n)")
                                ).then_inc(raw_in[j], 16)
                for r, (rows, prompt, sample) in enumerate(((k_rows, k.new_k_prompt, k.new_k_sample),
                                                            (v_rows, k.new_v_prompt, k.new_v_sample))):
                    e.wait_ge(rows_free, i * 2 + (r + 1))
                    e.dma_start(prompt[0, 0].rearrange("(b p) h d -> p b h d", p=P)[:, :, ds(i, 1), :],
                                rows[:, 0:4, :].unsqueeze(2)).then_inc(rows_stored[r], 16)
                    e.dma_start(sample[0].rearrange("b t h d -> (b t) h d")[:, ds(i, 1), :],
                                rows[0:NS, 4, :].unsqueeze(1)).then_inc(rows_stored[r], 16)
            for r in range(2):
                e.wait_ge(rows_stored[r], 32 * (NH + 1))

        @block.tensor
        def _(e):
            e.wait_ge(lam_a, 1)
            e.matmul(ss[:, 0, 0:2], k.c("ones")[0:DK, :], lam_prod[:], start=True, stop=True).then_inc(lam_b, 1)
            e.wait_ge(zero_lam, 1)
            with e.Fori(0, NH) as i:
                for j in range(2):
                    e.wait_ge(sq_ready, i * 2 + (j + 1))
                    e.wait_ge(qk_ready, i * 2 + (j + 1))
                    for h in range(2):
                        mm = e.matmul(ss[:, h, 0:HALF], k.c("block_ones"), sq[:, h * HALF:(h + 1) * HALF],
                                      start=True, stop=True)
                    mm.then_inc(ss_ready, 1)
                    e.wait_ge(normed_ready, i * 2 + (j + 1))
                    for h in range(2):
                        mm = e.matmul(ss[:, h, 0:HALF], k.c("rot"), normed[:, h * HALF:(h + 1) * HALF],
                                      start=True, stop=True)
                    mm.then_inc(rot_ready, 1)
                for r, src in enumerate((qk[:, 1, :], raw[:, 2, :])):
                    if r == 0:
                        e.wait_ge(qk_ready, i * 2 + 3)
                    else:
                        e.wait_ge(raw_in[2], i * 16 + 16)
                    e.wait_ge(tp_free, i * 2 + (r + 1))
                    for b in range(TB):
                        n = P if b < 4 else NS
                        mm = e.transpose(tp[0:n, b // 4, (b % 4) * P:(b % 4) * P + P], src[:, b * P:b * P + n], k.c("ident"))
                    mm.then_inc(tp_ready, 1)

                def scores(b):
                    if b:
                        e.wait_ge(e_ready, i * 8 + 2 * b)
                    for m in range(2):
                        r = slice(m * DK, (m + 1) * DK)
                        e.matmul(S[:, m, 0:(b + 1) * P], qk[r, 0, b * P:(b + 1) * P], qk[r, 1, 0:(b + 1) * P],
                                 start=True, stop=True).then_inc(S_ready, 1)

                scores(0)
                for b in range(4):
                    if b < 3:
                        scores(b + 1)
                    e.wait_ge(w_ready, i * 4 + (b + 1))
                    e.wait_ge(wT_ready, i * 4 + (b + 1))
                    for kb in range(b + 1):
                        mm = e.transpose(tw[:, kb, :], e_buf[:, b % 2, 0, kb * P:(kb + 1) * P], k.c("ident"))
                    mm.then_inc(tw_ready, 1)
                    e.wait_ge(wT_ready, i * 4 + (b + 2))
                    if b == 0:
                        e.wait_ge(tp_free, i * 2 + 3)
                        e.wait_ge(o_free, i + 1)
                    for kb in range(b + 1):
                        mm = e.matmul(o[:, b * P:(b + 1) * P], v_rows[:, kb, :], wT[:, b % 2, kb, :],
                                      start=kb == 0, stop=kb == b)
                    mm.then_inc(pv_done, 1)

        @block.scalar
        def _(e):
            e.wait_ge(lam_b, 1)
            e.activation(lam_exp[:], ss[:, 0, 0:2], ACT.Exp).then_inc(lam_c, 1)
            e.sem_inc(tp_free, 2 - 1)
            e.sem_inc(wT_ready, 1)
            e.sem_inc(o_free, 1)
            with e.Fori(0, NH) as i:
                for j in range(2):
                    e.wait_ge(raw_in[j], i * 16 + 16)
                    e.activation(sq[:], raw[:, j, :], ACT.Square).then_inc(sq_ready, 1)
                    e.wait_ge(ss_ready, i * 2 + (j + 1))
                    e.activation(halves(dev[:]), ss[:, :, 0:HALF], ACT.Sqrt, scale=1.0 / DK,
                                 bias=k.c("eps")).then_inc(dev_ready, 1)
                for r, rows in enumerate((k_rows, v_rows)):
                    e.wait_ge(tp_ready, i * 2 + (r + 1))
                    e.wait_ge(rows_stored[r], i * 32 + 32)
                    if r == 1:
                        e.wait_ge(pv_done, i * 4 + 4)
                    e.activation(rows[:, 0:4, :], tp[:, 0, :].rearrange("p (b n) -> p b n", b=4), ACT.Copy)
                    e.activation(rows[0:NS, 4, :], tp[0:NS, 1, 0:P], ACT.Copy).then_inc(tp_free, 1)
                    e.wait_ge(tp_free, i * 2 + (r + 2))
                    e.sem_inc(rows_free, 1)
                for b in range(4):
                    for m in range(2):
                        e.wait_ge(S_max, i * 8 + (2 * b + m + 1))
                        e.activation(e_buf[:, b % 2, m, 0:(b + 1) * P], S[:, m, 0:(b + 1) * P], ACT.Exp, scale=SCALE,
                                     bias=stat[:, b % 2, 2 + m:3 + m],
                                     accum_out=stat[:, b % 2, 4 + m:5 + m]).then_inc(e_ready, 1)
                    e.wait_ge(tw_ready, i * 4 + (b + 1))
                    if b >= 2:
                        e.wait_ge(pv_done, i * 4 + (b + 3))
                    e.activation(wT[:, b % 2, 0:b + 1, :], tw[:, 0:b + 1, :], ACT.Copy).then_inc(wT_ready, 1)
                e.wait_ge(pv_done, i * 4 + 8)
                e.activation(k.o[:, ds(i, 1), 0:NP].rearrange("p o n -> p (o n)"), o[:], ACT.Copy).then_inc(o_free, 1)

        @block.vector
        def _(e):
            ch = Chain(e, chain_sem)
            e.wait_ge(par_in, 16 * 6)
            e.tensor_tensor(lam_prod[:], lam_in[:, 0, :], lam_in[:, 1, :], ALU.mult).then_inc(lam_a, 1)
            e.wait_ge(lam_c, 1)
            ch.step(e.tensor_tensor(k.neg_lam[:], lam_exp[:, 1:2], lam_exp[:, 0:1], ALU.subtract))
            e.tensor_scalar(k.neg_lam[:], k.neg_lam[:], -LAM_INIT, None, ALU.add).then_inc(zero_lam, 1)
            e.wait_ge(zero_lam, 1)
            e.sem_inc(qk_ready, 1)
            e.sem_inc(pv_done, 4)
            for j in range(3):
                e.sem_inc(raw_free[j], 1)
            with e.Fori(0, NH) as i:
                ch.begin(i, 38)
                for j in range(2):
                    e.wait_ge(dev_ready, i * 2 + (j + 1))
                    ch.step(e.reciprocal(rstd[:], dev[:]))
                    e.scalar_tensor_tensor(out=normed[:], in0=raw[:, j, :], scalar=gains[:, j:j + 1], in1=rstd[:],
                                           op0=ALU.mult, op1=ALU.mult).then_inc(normed_ready, 1)
                    e.wait_ge(normed_ready, i * 2 + (j + 1))
                    e.sem_inc(raw_free[j], 1)
                    if j == 0:
                        e.wait_ge(pv_done, i * 4 + 4)
                    e.wait_ge(rot_ready, i * 2 + (j + 1))
                    ch.did(e.tensor_tensor(halves(turn[:]), ss[:, :, 0:HALF], halves(k.c("sin")), ALU.mult))
                    ch.step(e.tensor_tensor(qk[:, j, :], normed[:], k.c("cos"), ALU.mult))
                    ch.step(e.tensor_tensor(qk[:, j, :], qk[:, j, :], turn[:], ALU.add))
                    ch.step(e.tensor_copy(k.qk_sample[:, j, ds(i, 1), :], qk[:, j:j + 1, NP:TOK]))
                    e.sem_inc(qk_ready, 1)
                for b in range(4):
                    n = (b + 1) * P
                    st = stat[:, b % 2, :]
                    for m in range(2):
                        e.wait_ge(S_ready, i * 8 + (2 * b + m + 1))
                        ch.step(e.tensor_tensor(S[:, m, n - P:n], S[:, m, n - P:n], k.c("causal"), ALU.add))
                        ch.step(e.tensor_reduce(st[:, m:m + 1], S[:, m, 0:n], AX.X, ALU.max))
                        e.tensor_scalar(st[:, 2 + m:3 + m], st[:, m:m + 1], -SCALE, None, ALU.mult).then_inc(S_max, 1)
                    e.wait_ge(e_ready, i * 8 + (2 * b + 2))
                    ch.step(e.reciprocal(st[:, 6:8], st[:, 4:6]))
                    ch.did(e.tensor_tensor(st[:, 7:8], st[:, 7:8], k.neg_lam[:], ALU.mult))
                    ch.step(e.tensor_scalar(e_buf[:, b % 2, 0, 0:n], e_buf[:, b % 2, 0, 0:n], st[:, 6:7], None, ALU.mult))
                    e.scalar_tensor_tensor(out=e_buf[:, b % 2, 0, 0:n], in0=e_buf[:, b % 2, 1, 0:n], scalar=st[:, 7:8],
                                           in1=e_buf[:, b % 2, 0, 0:n], op0=ALU.mult, op1=ALU.add).then_inc(w_ready, 1)
                e.wait_ge(tp_ready, i * 2 + 2)
                e.sem_inc(raw_free[2], 1)
            ch.end(NH)


def stage_attention_sample(k):
    nc = k.nc
    R = 2 * NS
    with Space(nc, "dec") as s:
        table = s.sb("table", [1, NB * NPG], I32)
        K_ = s.sb("K", [P, 2, NPG, NH * P])
        V_ = s.sb("V", [P, 2, NPG, NH * P])
        v_new = s.sb("v_new", [NQ, 2, NH * P])
        q_wide = s.sb("q_wide", [P, NH * (2 * NQ + R)])
        kT = s.sb("kT", [P, 2, NPG * P])
        ex = s.sb("ex", [R, PAST + NQ])
        stat = s.sb("stat", [R, 8])
        sign = s.sb("sign", [R, 1])
        pick = s.sb("pick", [R, NS])
        wT = s.sb("wT", [P, NPG + 1, NS])
        kp = s.ps("kp", [P, 2, 2, 512])
        S = s.ps("S", [R, 2, 512])
        N = s.ps("N", [P, 512])
        S_new, W, O = N[0:R, 0:NQ], N[:, 64:64 + (NPG + 1) * NS], N[:, 480:480 + NH * NQ]
        W = N[:, 64:64 + (NPG + 1) * NS].rearrange("p (g n) -> p g n", n=NS)
        table_in = s.sem("table_in")
        k_in, v_in, vn_in = s.sems("k_in", 2), s.sems("v_in", 2), s.sems("vn_in", 2)
        k_used, pv_used = s.sem("k_used"), s.sem("pv_used")
        q_zero, q_ready = s.sem("q_zero"), s.sem("q_ready")
        kp_ready, kT_a, kT_v, s_used = s.sem("kp_ready"), s.sem("kT_a"), s.sem("kT_v"), s.sem("s_used")
        bias_ready, ex_ready, pick_ready, W_ready, wT_ready, O_ready, O_free = (
            s.sem(x) for x in ("bias_ready", "ex_ready", "pick_ready", "W_ready", "wT_ready", "O_ready", "O_free"))
        chain_sem = s.sem("chain")
        block = s.block()
        SCALE = DK ** -0.5

        @block.sync
        def _(e):
            e.dma_start(table[:], k.page_table.rearrange("b g -> (b g)").rearrange("(o n) -> o n", o=1)
                        ).then_inc(table_in, 16)
            e.wait_ge(table_in, 16)
            with e.Fori(0, NB // 2) as i:
                for b in range(2):
                    pages = [e.value_load(table[0:1, ds(i * (2 * NPG) + (b * NPG + g), 1)], min_val=0,
                                          max_val=k.cache_k.shape[1] - 1) for g in range(NPG)]
                    e.wait_ge(k_used, i * 2 + (b + 1))
                    for g in range(NPG):
                        e.dma_start(K_[:, b, g, :].unsqueeze(1),
                                    k.cache_k[0, ds(pages[g], 1)].rearrange("o p h d -> p o (h d)")).then_inc(k_in[b], 16)
                    e.wait_ge(pv_used, i * 2 + (b + 1))
                    for g in range(NPG):
                        e.dma_start(V_[:, b, g, :].unsqueeze(1),
                                    k.cache_v[0, ds(pages[g], 1)].rearrange("o p h d -> p o (h d)")).then_inc(v_in[b], 16)
                    e.dma_start(v_new[:, b, :].unsqueeze(1),
                                k.new_v_sample[0, ds(i * 2 + b, 1)].rearrange("o t h d -> t o (h d)")).then_inc(vn_in[b], 16)

        @block.gpsimd
        def _(e):
            e.memset(q_wide[:], 0.0).then_inc(q_zero, 1)

        @block.tensor
        def _(e):
            e.sem_inc(k_used, 2)
            e.sem_inc(pv_used, 2)
            with e.Fori(0, NB // 2) as i:
                for b in range(2):
                    n = i * 2 + b
                    e.wait_ge(k_in[b], i * (16 * NPG) + 16 * NPG)

                    def turn(h):
                        u = b * NH + h
                        e.wait_ge(kT_a, i * (2 * NH) + (u + 1))
                        e.wait_ge(kT_v, i * (2 * NH) + (u + 1))
                        for g in range(NPG):
                            mm = e.transpose(kp[:, h % 2, g // 4, (g % 4) * P:(g % 4 + 1) * P],
                                             K_[:, b, g, h * P:(h + 1) * P], k.c("ident"))
                        mm.then_inc(kp_ready, 1)

                    turn(0)
                    e.wait_ge(q_ready, n + 1)
                    for h in range(NH):
                        if h + 1 < NH:
                            turn(h + 1)
                        u = b * NH + h
                        lhs = q_wide[:, h * R:h * R + R]
                        e.wait_ge(kT_a, i * (2 * NH) + (u + 3))
                        e.matmul(S[:, 0, :], lhs, kT[:, h % 2, 0:512], start=h == 0, stop=h == NH - 1)
                        e.wait_ge(kT_v, i * (2 * NH) + (u + 3))
                        e.matmul(S[:, 1, :], lhs, kT[:, h % 2, 512:1024], start=h == 0, stop=h == NH - 1)
                        e.matmul(S_new, lhs, k.qk_sample[:, 1, h, ds(n * NQ, NQ)], start=h == 0,
                                 stop=h == NH - 1).then_inc(s_used, 1)
                    e.wait_ge(pick_ready, n + 1)
                    for g in range(NPG):
                        e.matmul(W[:, g, :], ex[:, g * P:(g + 1) * P], pick[:], start=True, stop=True)
                    e.matmul(W[0:NQ, NPG, :], ex[:, PAST:PAST + NQ], pick[:], start=True, stop=True).then_inc(W_ready, 1)
                    e.wait_ge(wT_ready, n + 1)
                    e.wait_ge(v_in[b], i * (16 * NPG) + 16 * NPG)
                    e.wait_ge(vn_in[b], i * 16 + 16)
                    for h in range(NH):
                        for g in range(NPG):
                            e.matmul(O[:, h * NQ:(h + 1) * NQ], V_[:, b, g, h * P:(h + 1) * P],
                                     wT[:, g, h * NQ:(h + 1) * NQ], start=g == 0, stop=False)
                        mm = e.matmul(O[:, h * NQ:(h + 1) * NQ], v_new[:, b, h * P:(h + 1) * P],
                                      wT[0:NQ, NPG, h * NQ:(h + 1) * NQ], start=False, stop=True)
                    mm.then_inc(pv_used, 1)
                    e.wait_ge(O_free, n + 1)

        @block.scalar
        def _(e):
            e.sem_inc(kT_a, 2)
            with e.Fori(0, NB // 2) as i:
                for b in range(2):
                    n = i * 2 + b
                    for h in range(NH):
                        u = b * NH + h
                        e.wait_ge(kp_ready, i * (2 * NH) + (u + 1))
                        if h >= 2:
                            e.wait_ge(s_used, i * (2 * NH) + (u - 1))
                        e.activation(kT[:, h % 2, 0:512], kp[:, h % 2, 0, :], ACT.Copy).then_inc(kT_a, 1)
                    e.wait_ge(bias_ready, n + 1)
                    e.activation(ex[:, 0:PAST].rearrange("p (a n) -> p a n", a=2), S[:], ACT.Exp, scale=SCALE,
                                 bias=stat[:, 3:4], accum_out=stat[:, 4:5]).then_inc(ex_ready, 1)
                    e.activation(ex[:, PAST:PAST + NQ], S_new, ACT.Exp, scale=SCALE, bias=stat[:, 3:4],
                                 accum_out=stat[:, 5:6]).then_inc(ex_ready, 1)
                    e.wait_ge(W_ready, n + 1)
                    e.activation(wT[:, 0:NPG, :], W[:, 0:NPG, :], ACT.Copy).then_inc(O_ready, 1)
                    e.activation(wT[0:NQ, NPG, :], W[0:NQ, NPG, :], ACT.Copy).then_inc(O_ready, 1)
                    e.wait_ge(O_ready, n * 2 + 2)
                    e.sem_inc(wT_ready, 1)

        @block.vector
        def _(e):
            ch = Chain(e, chain_sem)
            e.sem_inc(kT_v, 2)
            ch.step(e.tensor_tensor(sign[:], k.c("map_two")[0:R, :], k.neg_lam[0:R, :], ALU.mult))
            ch.step(e.tensor_tensor(sign[:], sign[:], k.c("map_one")[0:R, :], ALU.add))
            e.wait_ge(q_zero, 1)
            with e.Fori(0, NB // 2) as i:
                ch.begin(i, 2 * 10)
                for b in range(2):
                    n = i * 2 + b
                    view = q_wide[:].rearrange("p (h c) -> p h c", c=R + 2 * NQ)
                    for m in range(2):
                        r = slice(m * DK, (m + 1) * DK)
                        ins = e.tensor_copy(view[r, :, m * NQ:(m + 1) * NQ], k.qk_sample[r, 0, :, ds(n * NQ, NQ)])
                        ch.did(ins)
                    ch.wait()
                    e.sem_inc(q_ready, 1)
                    for h in range(NH):
                        u = b * NH + h
                        e.wait_ge(kp_ready, i * (2 * NH) + (u + 1))
                        if h >= 2:
                            e.wait_ge(s_used, i * (2 * NH) + (u - 1))
                        e.tensor_copy(kT[:, h % 2, 512:1024], kp[:, h % 2, 1, :]).then_inc(kT_v, 1)
                    e.wait_ge(s_used, i * (2 * NH) + (b * NH + NH))
                    e.sem_inc(k_used, 1)
                    ch.did(e.tensor_tensor(S_new, S_new, k.c("sample_mask")[0:R, :], ALU.add))
                    ch.step(e.tensor_reduce(stat[:, 0:1], S[:], AX.XY, ALU.max))
                    ch.step(e.tensor_reduce(stat[:, 1:2], S_new, AX.X, ALU.max))
                    ch.step(e.tensor_tensor(stat[:, 2:3], stat[:, 0:1], stat[:, 1:2], ALU.max))
                    e.tensor_scalar(stat[:, 3:4], stat[:, 2:3], -SCALE, None, ALU.mult).then_inc(bias_ready, 1)
                    e.wait_ge(ex_ready, n * 2 + 2)
                    ch.step(e.tensor_tensor(stat[:, 6:7], stat[:, 4:5], stat[:, 5:6], ALU.add))
                    ch.step(e.reciprocal(stat[:, 6:7], stat[:, 6:7]))
                    ch.step(e.tensor_tensor(stat[:, 7:8], stat[:, 6:7], sign[:], ALU.mult))
                    e.tensor_scalar(pick[:], k.c("pair_sum")[0:R, :], stat[:, 7:8], None, ALU.mult).then_inc(pick_ready, 1)
                    e.wait_ge(pv_used, n + 3)
                    ch.step(e.tensor_copy(k.o[:, :, ds(n * NQ + NP, NQ)], O.rearrange("p (h q) -> p h q", h=NH)))
                    e.sem_inc(O_free, 1)
            ch.end(NB // 2)


def stage_attention_norm(k):
    nc = k.nc
    with Space(nc, "hnorm") as s:
        sq = s.sb("sq", [P, TOK])
        dev = s.sb("dev", [P, TOK])
        rstd = s.sb("rstd", [P, TOK])
        gain = s.sb("gain", [P, 2])
        scaled = s.sb("scaled", [P, TOK])
        ss = s.ps("ss", [P, 2, 512])
        gain_in, gain_ready, sq_ready, ss_ready, dev_ready, scaled_ready, hi_ready, done = (
            s.sem(x) for x in ("gain_in", "gain_ready", "sq_ready", "ss_ready", "dev_ready", "scaled_ready",
                               "hi_ready", "done"))
        chain_sem = s.sem("chain")
        block = s.block()

        @block.sync
        def _(e):
            e.dma_start(gain[:, 0:1], k.g_head[0].rearrange("(p o) -> p o", o=1),
                        allow_slow_non_contiguous=True).then_inc(gain_in, 16)

        @block.scalar
        def _(e):
            with e.Fori(0, NH) as i:
                e.activation(sq[:], k.o[:, ds(i, 1), :].rearrange("p o n -> p (o n)"), ACT.Square).then_inc(sq_ready, 1)
                e.wait_ge(ss_ready, i + 1)
                e.activation(halves(dev[:]), ss[:, :, 0:HALF], ACT.Sqrt, scale=1.0 / DV, bias=k.c("eps")).then_inc(dev_ready, 1)
                e.wait_ge(scaled_ready, i + 1)
                e.activation(k.att[:, ds(i, 1), 0, :].rearrange("p o n -> p (o n)"), scaled[:], ACT.Copy).then_inc(hi_ready, 1)

        @block.tensor
        def _(e):
            with e.Fori(0, NH) as i:
                e.wait_ge(sq_ready, i + 1)
                for h in range(2):
                    mm = e.matmul(ss[:, h, 0:HALF], k.c("ones"), sq[:, h * HALF:(h + 1) * HALF], start=True, stop=True)
                mm.then_inc(ss_ready, 1)

        @block.vector
        def _(e):
            ch = Chain(e, chain_sem)
            e.wait_ge(gain_in, 16)
            ch.step(e.tensor_scalar(gain[:, 1:2], gain[:, 0:1], 1.0 - LAM_INIT, None, ALU.mult))
            with e.Fori(0, NH) as i:
                ch.begin(i, 1)
                e.wait_ge(dev_ready, i + 1)
                ch.step(e.reciprocal(rstd[:], dev[:]))
                e.scalar_tensor_tensor(out=scaled[:], in0=k.o[:, ds(i, 1), :].rearrange("p o n -> p (o n)"),
                                       scalar=gain[:, 1:2], in1=rstd[:], op0=ALU.mult, op1=ALU.mult).then_inc(scaled_ready, 1)
                e.wait_ge(hi_ready, i + 1)
                e.tensor_tensor(k.att[:, ds(i, 1), 1, :].rearrange("p o n -> p (o n)"), scaled[:],
                                k.att[:, ds(i, 1), 0, :].rearrange("p o n -> p (o n)").bitcast(F32),
                                ALU.subtract).then_inc(done, 1)
                e.wait_ge(done, i + 1)
            ch.end(NH)


def stage_mix(k):
    nc = k.nc
    with Space(nc, "mix") as s:
        w = Stream(s)
        y_raw = s.sb("y_raw", [P, CT, TOK])
        ys = s.sb("ys", [P, CT, 2, TOK], F32R)
        gate = s.sb("gate", [P, 2, 2, TOK])
        a_part = s.sb("a_part", [P, TOK])
        sig = s.sb("sig", [P, TOK])
        b_part = s.sb("b_part", [P, TOK])
        mix = s.sb("mix", [P, 2, TOK])
        acc = [s.ps(f"acc{a}", [P, 2, 512]) for a in range(3)]
        y_in, y_hi, y_rest = s.sem("y_in"), s.sem("y_hi"), s.sem("y_rest")
        gate_in, gate_free = s.sems("gate_in", 2), s.sem("gate_free")
        a_read, v_read, g_read, mix_ready = s.sem("a_read"), s.sem("v_read"), s.sem("g_read"), s.sem("mix_ready")
        mix_stored = s.sems("mix_stored", 2)
        chain_sem = s.sem("chain")
        block = s.block()
        U = CT // UNIT
        PC = 3 * U
        PER = 2 * PC
        N = KT // 2

        def src(i, a, u):
            part, kt0 = u // U, UNIT * (u % U)
            col = i * (2 * P) + a * P
            if part == 0:
                return columns(k.w_attn_up[0], col, kt0)
            return columns(k.w_glu[0], col if part == 1 else col + D_MODEL, kt0)

        @block.sync
        def _(e):
            e.dma_start(y_raw[:], k.y_dram.rearrange("t p n -> p t n")).then_inc(y_in, 16)
            with e.Fori(0, N) as i:
                for a in range(2):
                    for u in range(PC):
                        w.load(e, i, PER, a * PC + u, src(i, a, u))
                        if u == 1:
                            e.wait_ge(gate_free, i * 2 + (a + 1))
                            for g in range(2):
                                e.dma_start(gate[:, a, g, :], k.z_dram[ds(i * 2 + (24 + KT * g + a), 1)]
                                            .rearrange("o p n -> p (o n)")).then_inc(gate_in[a], 16)

        @block.gpsimd
        def _(e):
            w.credit_rest(e)
            with e.Fori(0, N) as i:
                for u in range(PER):
                    w.split_rest(e, i, PER, u)

        @block.tensor
        def _(e):
            w.credit_used(e)
            e.wait_ge(y_rest, CT)
            with e.Fori(0, N) as i:
                for a in range(2):
                    for part, (read, moving) in enumerate(((a_read, k.att), (v_read, ys), (g_read, ys))):
                        e.wait_ge(read, i * 2 + (a + 1))
                        for u in range(U):
                            w.multiply(e, i, PER, a * PC + part * U + u, acc[part], moving, u * UNIT,
                                       u == 0, u == U - 1)

        @block.scalar
        def _(e):
            e.sem_inc(g_read, 1)
            e.sem_inc(mix_stored[0], 16)
            e.sem_inc(mix_stored[1], 16)
            e.wait_ge(y_in, 16)
            for t in range(CT):
                e.activation(ys[:, t, 0, :], y_raw[:, t, :], ACT.Copy).then_inc(y_hi, 1)

            def finish(i, a):
                w.wait_used(e, i, PER, (a + 1) * PC)
                e.wait_ge(v_read, i * 2 + (a + 1))
                e.activation(halves(sig[:]), acc[2][:, :, 0:HALF], ACT.Sigmoid).then_inc(g_read, 1)

            def store(i, a):
                e.wait_ge(mix_ready, i * 2 + (a + 1))
                e.dma_start(k.mix_dram[ds(i * 2 + a, 1)].rearrange("o p n -> p (o n)"),
                            mix[:, a, :]).then_inc(mix_stored[a], 16)

            def body(i, first):
                for a in range(2):
                    for u in range(PC):
                        w.split_hi(e, i, PER, a * PC + u)
                        if u == 2:
                            if a == 1:
                                finish(i, 0)
                            elif not first:
                                finish(i - 1, 1)
                        if u == PC - 1:
                            if a == 1:
                                store(i, 0)
                            elif not first:
                                store(i - 1, 1)

            body(0, True)
            with e.Fori(1, N) as i:
                body(i, False)
            finish(N - 1, 1)
            store(N - 1, 1)
            for a in range(2):
                e.wait_ge(mix_stored[a], 16 * (N + 1))

        @block.vector
        def _(e):
            ch = Chain(e, chain_sem)
            e.sem_inc(a_read, 1)
            e.sem_inc(v_read, 1)
            e.sem_inc(gate_free, 2)
            for t in range(CT):
                e.wait_ge(y_hi, t + 1)
                e.tensor_tensor(ys[:, t, 1, :], y_raw[:, t, :], ys[:, t, 0, :].bitcast(F32),
                                ALU.subtract).then_inc(y_rest, 1)
            with e.Fori(0, N) as i:
                ch.begin(i, 2 * 2)
                for a in range(2):
                    w.wait_used(e, i, PER, a * PC + U)
                    e.wait_ge(gate_in[a], i * 32 + 32)
                    e.tensor_tensor(halves(a_part[:]), acc[0][:, :, 0:HALF], halves(gate[:, a, 0, :]),
                                    ALU.mult).then_inc(a_read, 1)
                    e.wait_ge(g_read, i * 2 + (a + 2))
                    ch.step(e.tensor_tensor(halves(b_part[:]), acc[1][:, :, 0:HALF], halves(sig[:]), ALU.mult))
                    e.sem_inc(v_read, 1)
                    ch.step(e.tensor_tensor(b_part[:], b_part[:], gate[:, a, 1, :], ALU.mult))
                    e.wait_ge(a_read, i * 2 + (a + 2))
                    e.sem_inc(gate_free, 1)
                    e.wait_ge(mix_stored[a], i * 16 + 16)
                    e.tensor_tensor(mix[:, a, :], a_part[:], b_part[:], ALU.add).then_inc(mix_ready, 1)
                    e.wait_ge(mix_ready, i * 2 + (a + 1))
            ch.end(N)


def stage_out(k):
    nc = k.nc
    with Space(nc, "wout") as s:
        w = Stream(s)
        raw = s.sb("raw", [P, 4, TOK])
        acc = [s.ps(f"acc{a}", [P, 2, 512]) for a in range(2)]
        x_in, raw_in, hi_ready, rest_ready = s.sem("x_in"), s.sems("raw_in", 4), s.sem("hi_ready"), s.sem("rest_ready")
        acc_free = s.sem("acc_free")
        block = s.block()
        U = KT // UNIT
        PER = 2 * U

        @block.sync
        def _(e):
            for t in range(KT):
                if t >= 4:
                    e.wait_ge(rest_ready, t - 3)
                e.dma_start(raw[:, t % 4, :], k.mix_dram[t]).then_inc(raw_in[t % 4], 16)
                if t == 3:
                    for u in range(RING):
                        w.load(e, 0, PER, u, columns(k.w_out[0], 0, UNIT * u))
            e.dma_start(k.xT[:], k.xT_dram).then_inc(x_in, 16)
            for u in range(RING, PER):
                w.load(e, 0, PER, u, columns(k.w_out[0], P * (u // U), UNIT * (u % U)))
            with e.Fori(1, KT // 2) as i:
                for u in range(PER):
                    w.load(e, i, PER, u, columns(k.w_out[0], i * (2 * P) + P * (u // U), UNIT * (u % U)))

        @block.gpsimd
        def _(e):
            w.credit_rest(e)
            with e.Fori(0, KT // 2) as i:
                for u in range(PER):
                    w.split_rest(e, i, PER, u)

        @block.scalar
        def _(e):
            for t in range(KT):
                e.wait_ge(raw_in[t % 4], 16 * (t // 4 + 1))
                e.activation(k.act[:, t, 0, :], raw[:, t % 4, :], ACT.Copy).then_inc(hi_ready, 1)
            with e.Fori(0, KT // 2) as i:
                for u in range(PER):
                    w.split_hi(e, i, PER, u)

        @block.tensor
        def _(e):
            w.credit_used(e)
            e.wait_ge(rest_ready, KT)
            with e.Fori(0, KT // 2) as i:
                for a in range(2):
                    e.wait_ge(acc_free, i * 2 + (a + 1))
                    for u in range(U):
                        w.multiply(e, i, PER, a * U + u, acc[a], k.act, u * UNIT, u == 0, u == U - 1)

        @block.vector
        def _(e):
            e.sem_inc(acc_free, 2)
            for t in range(KT):
                e.wait_ge(hi_ready, t + 1)
                e.tensor_tensor(k.act[:, t, 1, :], raw[:, t % 4, :], k.act[:, t, 0, :].bitcast(F32),
                                ALU.subtract).then_inc(rest_ready, 1)
            e.wait_ge(x_in, 16)
            with e.Fori(0, KT // 2) as i:
                for a in range(2):
                    w.wait_used(e, i, PER, (a + 1) * U)
                    x = k.xT[:, ds(i * 2 + a, 1), :].rearrange("p o (a n) -> p (o a) n", a=2)
                    e.tensor_tensor(x, x, acc[a][:, :, 0:HALF], ALU.add).then_inc(acc_free, 1)


def stage_norm(k, gain, tag):
    with Space(k.nc, tag) as s:
        norm = Norm(s, k.xT, gain, k.act, k.c)
        block = s.block()

        @block.sync
        def _(e):
            norm.load(e)

        @block.scalar
        def _(e):
            norm.scalar(e)

        @block.tensor
        def _(e):
            norm.tensor(e)

        @block.vector
        def _(e):
            norm.vector(e)


def stage_route(k):
    nc = k.nc
    with Space(nc, "route") as s:
        w = Stream(s)
        keys = s.sb("keys", [P, 2, P])
        keysT = s.sb("keysT", [P, 2, P])
        q = s.sb("q", [P, 2, TOK])
        scores = s.sb("scores", [P, TB, P])
        rest = s.sb("rest", [P, 2 * P])
        val = s.sb("val", [P, TB, 2, TOPK])
        cand = s.sb("cand", [P, TOPK, TOPK])
        idx = s.sb("idx", [P, TB, 2, TOPK], U32)
        best = s.sb("best", [P, TB, TOPK])
        at = s.sb("at", [P, TB, TOPK], U32)
        acc = [s.ps(f"acc{a}", [P, 2, 512]) for a in range(2)]
        sc = s.ps("sc", [P, 2, 512])
        tp = s.ps("tp", [P, 2, 512])
        keys_in, keys_turned, keys_ready = s.sem("keys_in"), s.sem("keys_turned"), s.sem("keys_ready")
        acc_free, q_ready, q_used, sc_ready, sc_free = (s.sem(x) for x in
                                                        ("acc_free", "q_ready", "q_used", "sc_ready", "sc_free"))
        chain_sem = s.sem("chain")
        block = s.block()
        U = KT // UNIT
        PER = 2 * U
        N = KT // 2

        @block.sync
        def _(e):
            e.dma_start(keys[:], k.peer_sub_keys[0].rearrange("m k d -> k m d")).then_inc(keys_in, 16)
            with e.Fori(0, N) as i:
                for u in range(PER):
                    w.load(e, i, PER, u, columns(k.peer_w_query[0], i * (2 * P) + P * (u // U), UNIT * (u % U)))

        @block.gpsimd
        def _(e):
            w.credit_rest(e)
            with e.Fori(0, N) as i:
                for u in range(PER):
                    w.split_rest(e, i, PER, u)

        @block.scalar
        def _(e):
            e.sem_inc(acc_free, 2)

            def query_out(i, a):
                w.wait_used(e, i, PER, (a + 1) * U)
                e.wait_ge(q_used, i * 2 + (a + 1))
                e.activation(halves(q[:, a, :]), acc[a][:, :, 0:HALF], ACT.Copy).then_inc(q_ready, 1)
                e.wait_ge(q_ready, i * 2 + (a + 1))
                e.sem_inc(acc_free, 1)

            def body(i, first):
                for a in range(2):
                    for u in range(U):
                        w.split_hi(e, i, PER, a * U + u)
                    if a == 1:
                        query_out(i, 0)
                    elif not first:
                        query_out(i - 1, 1)

            body(0, True)
            with e.Fori(1, N) as i:
                body(i, False)
            query_out(N - 1, 1)

        @block.tensor
        def _(e):
            w.credit_used(e)
            e.sem_inc(q_used, 2)
            e.wait_ge(keys_in, 16)
            for m in range(2):
                e.transpose(tp[:, m, 0:P], keys[:, m, :], k.c("ident")).then_inc(keys_turned, 1)
            e.wait_ge(keys_ready, 1)

            def score(i, a):
                e.wait_ge(q_ready, i * 2 + (a + 1))
                e.wait_ge(sc_free, i * 2 + (a + 1))
                for b in range(TB):
                    n = P if b < 4 else NS
                    mm = e.matmul(sc[0:n, b // 4, (b % 4) * P:(b % 4 + 1) * P], q[:, a, b * P:b * P + n], keysT[:, a, :],
                                  start=True, stop=True)
                mm.then_inc(q_used, 1)

            def body(i, first):
                for a in range(2):
                    e.wait_ge(acc_free, i * 2 + (a + 1))
                    for u in range(U):
                        w.multiply(e, i, PER, a * U + u, acc[a], k.act, u * UNIT, u == 0, u == U - 1)
                    if a == 1:
                        score(i, 0)
                    elif not first:
                        score(i - 1, 1)

            body(0, True)
            with e.Fori(1, N) as i:
                body(i, False)
            score(N - 1, 1)

        @block.vector
        def _(e):
            ch = Chain(e, chain_sem)
            e.sem_inc(sc_free, 1)
            ch.did(e.memset(idx[:, 4].bitcast(F32), 0.0))
            ch.did(e.memset(at[:, 4].bitcast(F32), 0.0))
            ch.did(e.memset(best[:, 4], 0.0))
            ch.wait()
            e.wait_ge(keys_turned, 2)
            e.tensor_copy(keysT[:], tp[:, :, 0:P]).then_inc(keys_ready, 1)
            with e.Fori(0, N) as i:
                ch.begin(i, 2 * (2 + TB * 5) + TB * 6 + 3)
                for m in range(2):
                    e.wait_ge(q_used, i * 2 + (m + 3))
                    ch.did(e.tensor_copy(scores[:, 0:4, :], sc[:, 0, :].rearrange("p (b n) -> p b n", b=4)))
                    ch.step(e.tensor_copy(scores[0:NS, 4, :], sc[0:NS, 1, 0:P]))
                    e.sem_inc(sc_free, 1)
                    for b in range(TB):
                        r = slice(0, P if b < 4 else NS)
                        S, V = scores[r, b, :], val[r, b, m, :]
                        I = idx[r, b, m, :]
                        ch.step_apart(e.max(V[:, 0:8], S))
                        ch.did(e.max_index(I[:, 0:8], V[:, 0:8], S))
                        ch.step_apart(e.match_replace(rest[r, 0:P], V[:, 0:8], S, -3e38))
                        ch.step_apart(e.max(V[:, 8:16], rest[r, 0:P]))
                        ch.step_apart(e.max_index(I[:, 8:16], V[:, 8:16], rest[r, 0:P]))
                for b in range(TB):
                    r = slice(0, P if b < 4 else NS)
                    C = cand[r]
                    flat = C.rearrange("p a b -> p (a b)")
                    ch.step_apart(e.tensor_tensor(C, wide(val[r, b, 0, :], TOPK), turned(val[r, b, 1, :], TOPK), ALU.add))
                    V, I = best[r, b, :], at[r, b, :]
                    ch.step_apart(e.max(V[:, 0:8], flat))
                    ch.did(e.max_index(I[:, 0:8], V[:, 0:8], flat))
                    ch.step_apart(e.match_replace(rest[r, :], V[:, 0:8], flat, -3e38))
                    ch.step_apart(e.max(V[:, 8:16], rest[r, :]))
                    ch.step_apart(e.max_index(I[:, 8:16], V[:, 8:16], rest[r, :]))
                for whole, head in ((k.idx, idx[:].rearrange("p b m k -> p b (m k)")), (k.best, best[:]), (k.at, at[:])):
                    ch.did(e.tensor_copy(whole[:, :, ds(i, 1), :].rearrange("p b o n -> p b (o n)"), head))
                ch.wait()
            ch.end(N)


def stage_tables(k):
    nc = k.nc
    HK = NH * TOPK
    with Space(nc, "tabs") as s:
        half = s.sb("half", [P, 2, TB * HK], U32)
        half_f = s.sb("half_f", [P, 2, TB * HK])
        match = s.sb("match", [P, 2, NH, TOPK, TOPK])
        rows = s.sb("rows", [P, 3, TB, HK])
        e_sum = s.sb("e_sum", [P, TB, NH])
        tp = s.ps("tp", [P, 2, 512])
        shifted, exp_done, rows_done, turned_sem, copied = (s.sem(x) for x in
                                                            ("shifted", "exp_done", "rows_done", "turned", "copied"))
        chain_sem, pool_chain = s.sem("chain"), s.sem("pool_chain")
        found = s.sem("found")
        block = s.block()

        @block.vector
        def _(e):
            ch = Chain(e, chain_sem)
            for b in range(TB):
                best = k.best[:, b]
                ch.did(e.tensor_tensor(rows[:, 2, b, :].rearrange("p (h k) -> p h k", h=NH), best,
                                       best[:, :, 0:1].broadcast_to([P, NH, TOPK]), ALU.subtract))
            ch.wait()
            e.sem_inc(shifted, 1)
            flat = k.at[:].rearrange("p b h k -> p (b h k)")
            ch.did(e.tensor_single_scalar(half[:, 0, :], flat, 4, ALU.logical_shift_right))
            ch.step(e.tensor_single_scalar(half[:, 1, :], flat, 15, ALU.bitwise_and))
            ch.step(e.tensor_copy(half_f[:], half[:]))
            for b in range(TB):
                for m in range(2):
                    M = match[:, m]
                    flat_m = M.rearrange("p h k r -> p (h k) r")
                    ch.step(e.tensor_tensor(flat_m, wide(half_f[:, m, b * HK:(b + 1) * HK], TOPK),
                                            turned(k.c("iota16"), HK), ALU.is_equal))
                    ch.step(e.tensor_tensor(M, M, k.idx[:, b, :, m * TOPK:(m + 1) * TOPK].unsqueeze(2).broadcast_to([P, NH, TOPK, TOPK]),
                                            ALU.mult))
                    ch.step(e.tensor_reduce(rows[:, m, b, :], flat_m, AX.X, ALU.add))
            e.wait_ge(exp_done, 1)
            ch.step(e.tensor_reduce(e_sum[:], rows[:, 2].rearrange("p b (h k) -> p b h k", h=NH), AX.X, ALU.add))
            ch.step(e.reciprocal(e_sum[:], e_sum[:]))
            for b in range(TB):
                g = rows[:, 2, b, :].rearrange("p (h k) -> p h k", h=NH)
                ch.step(e.tensor_tensor(g, g, wide(e_sum[:, b, :], TOPK), ALU.mult))
            e.sem_inc(rows_done, 1)
            for t in range(3):
                e.wait_ge(turned_sem, t + 1)
                ch.did(e.tensor_copy(k.tables[:, t, 0:NP], tp[:, 0, :]))
                ch.did(e.tensor_copy(k.tables[:, t, NP:TOK], tp[:, 1, 0:NS]))
                ch.wait()
                e.sem_inc(copied, 1)

        @block.scalar
        def _(e):
            e.wait_ge(shifted, 1)
            e.activation(rows[:, 2], rows[:, 2], ACT.Exp).then_inc(exp_done, 1)

        @block.tensor
        def _(e):
            e.wait_ge(rows_done, 1)
            for t in range(3):
                if t:
                    e.wait_ge(copied, t)
                for b in range(TB):
                    n = P if b < 4 else NS
                    mm = e.transpose(tp[:, b // 4, (b % 4) * P:(b % 4) * P + n], rows[0:n, t, b, :], k.c("ident")[0:n, 0:n])
                mm.then_inc(turned_sem, 1)


def stage_gates(k):
    nc = k.nc
    CH, BT, Q = 64, 8, 4
    with Space(nc, "gate") as s:
        A = s.sb("A", [P, 2, BT, P])
        B = s.sb("B", [P, 2, BT, P])
        out = s.sb("out", [P, 2, PK, CH])
        ps = s.ps("ps", [P, 8, Q, P])
        A_ready, ps_ready, ps_free = (s.sem(x) for x in ("A_ready", "ps_ready", "ps_free"))
        stored = s.sems("stored", 2)
        block = s.block()
        NBATCH = CH // BT
        PER = 2 * NBATCH
        N = NP // (2 * CH)
        TAIL = NS // BT

        @block.vector
        def _(e):
            def batch(i, b):
                e.wait_ge(ps_ready, i * (PER * BT // Q) + (b + 1) * (BT // Q))
                n0 = i * (PER * BT) + b * BT
                e.tensor_tensor(B[:, b % 2], turned(k.c("iota"), BT), wide(k.tables[:, 1, ds(n0, BT)], P),
                                ALU.is_equal)
                for t in range(BT):
                    n = i * (PER * BT) + (b * BT + t)
                    ins = e.tensor_scalar(A[:, b % 2, t, :], k.c("iota"), k.tables[:, 0, ds(n, 1)],
                                          k.tables[:, 2, ds(n, 1)], ALU.is_equal, ALU.mult)
                ins.then_inc(A_ready, 1)

            with e.Fori(0, N) as i:
                for b in range(PER):
                    batch(i, b)
            for b in range(TAIL):
                batch(N, b)

        @block.tensor
        def _(e):
            e.sem_inc(ps_ready, 2 * BT // Q)

            def batch(i, b):
                e.wait_ge(A_ready, i * PER + (b + 1))
                for g in range(BT // Q):
                    u = b * (BT // Q) + g
                    e.wait_ge(ps_free, i * (PER * BT // Q) + (u + 1))
                    for t in range(Q):
                        mm = e.matmul(ps[:, u % 8, t, :], A[:, b % 2, g * Q + t, :], B[:, b % 2, g * Q + t, :],
                                      start=True, stop=True)
                    mm.then_inc(ps_ready, 1)

            with e.Fori(0, N) as i:
                for b in range(PER):
                    batch(i, b)
            for b in range(TAIL):
                batch(N, b)

        @block.scalar
        def _(e):
            e.sem_inc(ps_free, 8)
            e.sem_inc(stored[0], 16)
            e.sem_inc(stored[1], 16)

            def chunk(i, c, n):
                base = i * (PER * BT // Q)
                e.wait_ge(stored[c], i * 16 + 16)
                for g in range(n // Q):
                    u = c * (CH // Q) + g
                    e.wait_ge(ps_ready, base + (u + 1 + 2 * BT // Q))
                    e.activation(out[:, c, :, g * Q:(g + 1) * Q].rearrange("p j n -> p n j"), ps[:, u % 8],
                                 ACT.Copy).then_inc(ps_free, 1)
                e.wait_ge(ps_free, base + (c * (CH // Q) + n // Q + 8))
                e.dma_start(k.gate_dram[:, :, ds(i * (2 * CH) + c * CH, n)], out[:, c, :, 0:n]).then_inc(stored[c], 16)

            with e.Fori(0, N) as i:
                for c in range(2):
                    chunk(i, c, CH)
            chunk(N, 0, NS)
            e.wait_ge(stored[0], 16 * (N + 2))
            e.wait_ge(stored[1], 16 * (N + 1))


def stage_experts(k):
    nc = k.nc
    NPAIR = PK // 2
    CK = 4
    NC = KT // CK
    HC = NC // 2
    W = CK * P
    with Space(nc, "exp") as s:
        u_raw = s.sb("u_raw", [P, 4, W])
        uT = s.sb("uT", [P, 4, 2, CK, P], F32R)
        v_raw = s.sb("v_raw", [P, 2, 2, W])
        v = s.sb("v", [P, 2, 2, 2, W], F32R)
        gate = s.sb("gate", [P, 2, 2, TOK])
        hid = s.sb("hid", [P, 2, TOK])
        wt = s.sb("wt", [P, 2, 2, 2, TOK], F32R)
        tp = s.ps("tp", [P, 2, CK, P])
        h_ps = s.ps("h_ps", [P, 2, 512])
        y_ps = s.ps("y_ps", [P, 2, 2, 512])
        u_in, v_in, gate_in = s.sems("u_in", 4), s.sems("v_in", 2), s.sems("gate_in", 2)
        u_turned, uT_hi, uT_rest, uT_used = (s.sem(x) for x in ("u_turned", "uT_hi", "uT_rest", "uT_used"))
        v_hi, v_rest = s.sem("v_hi"), s.sem("v_rest")
        h_ready, gelu_done, gated, w_hi, w_rest = (s.sem(x) for x in ("h_ready", "gelu_done", "gated", "w_hi", "w_rest"))
        y_ready, y_added = s.sem("y_ready"), s.sem("y_added")
        block = s.block()
        u_dram = k.peer_u[0].rearrange("(i j) d -> i j d", j=PK)
        v_dram = k.peer_v[0].rearrange("(i j) d -> i j d", j=PK)

        def at(i, pp, per, plus):
            return i * (2 * per) + (pp * per + plus)

        def pipeline(e, part, rest):
            part(0, 0, 0, False, True)
            part(0, 0, 1, False, True)
            with e.Fori(0, NPAIR // 2 - 1) as i:
                for pp in (1, 2):
                    for j in range(2):
                        part(i, pp, j, True, True)
            part(NPAIR // 2 - 1, 1, 0, True, True)
            part(NPAIR // 2 - 1, 1, 1, True, False)
            rest(NPAIR // 2 - 1, 1)

        @block.sync
        def _(e):
            def load_v(i, pp, c):
                e.wait_ge(v_rest, at(i, pp, NC, c + 1))
                e.dma_start(v_raw[:, c % 2], v_dram[:, ds(i * 4 + 2 * pp, 2), c * W:(c + 1) * W]).then_inc(v_in[c % 2], 16)

            def part(i, pp, j, outputs, ahead):
                p = i * 2 + pp
                if outputs:
                    for c in range(HC):
                        load_v(i, pp - 1, j * HC + c)
                if j == 0:
                    e.wait_ge(gated, at(i, pp, 2, 1))
                    e.dma_start(gate[:, pp % 2], k.gate_dram[:, ds(p * 2, 2), :]).then_inc(gate_in[pp % 2], 16)
                for c in range(NC):
                    e.wait_ge(u_turned, at(i, pp, 2 * NC, j * NC + c + 1))
                    e.dma_start(u_raw[:, c, :].unsqueeze(1), u_dram[:, ds(p * 2 + j, 1), c * W:(c + 1) * W]
                                ).then_inc(u_in[c], 16)

            def rest(i, pp):
                for c in range(NC):
                    load_v(i, pp, c)

            pipeline(e, part, rest)

        @block.tensor
        def _(e):
            e.sem_inc(u_turned, 4)
            e.sem_inc(uT_used, 4)
            e.sem_inc(y_ready, KT)

            def turn(i, pp, j, c):
                pp, j = pp + j // 2, j % 2
                e.wait_ge(u_in[c], at(i, pp, 32, 16 * (j + 1)))
                e.wait_ge(uT_rest, at(i, pp, 2 * NC, j * NC + c + 1))
                for t in range(CK):
                    mm = e.transpose(tp[:, c % 2, t, :], u_raw[:, c, t * P:(t + 1) * P], k.c("ident"))
                mm.then_inc(u_turned, 1)

            def hidden(i, pp, j, c):
                e.wait_ge(uT_rest, at(i, pp, 2 * NC, j * NC + c + 3))
                for t in range(CK):
                    for a, b in ((0, 0), (0, 1), (1, 0)):
                        for h in range(2):
                            mm = e.matmul(h_ps[:, h, 0:HALF], uT[:, c, a, t, :],
                                          k.act[:, c * CK + t, b, h * HALF:(h + 1) * HALF],
                                          start=c == 0 and t == 0 and a == 0 and b == 0,
                                          stop=c == NC - 1 and t == CK - 1 and a == 1)
                mm.then_inc(uT_used, 1)

            def output(i, pp, c, tiles):
                if 0 in tiles:
                    e.wait_ge(v_rest, at(i, pp, NC, c + 3))
                    if c == 0:
                        e.wait_ge(w_rest, at(i, pp, 2, 4))
                for t in tiles:
                    e.wait_ge(y_added, at(i, pp, KT, c * CK + t + 1))
                    for j in range(2):
                        for a, b in ((0, 0), (0, 1), (1, 0)):
                            for h in range(2):
                                mm = e.matmul(y_ps[:, t % 2, h, 0:HALF], v[:, c % 2, a, j, t * P:(t + 1) * P],
                                              wt[:, pp % 2, j, b, h * HALF:(h + 1) * HALF],
                                              start=j == 0 and a == 0 and b == 0, stop=j == 1 and a == 1)
                    mm.then_inc(y_ready, 1)

            def part(i, pp, j, outputs, ahead):
                if not outputs and j == 0:
                    turn(i, pp, j, 0)
                    turn(i, pp, j, 1)
                e.wait_ge(gelu_done, at(i, pp, 2, j + 1))
                hidden(i, pp, j, 0)
                turn(i, pp, j, 2)
                hidden(i, pp, j, 1)
                turn(i, pp, j, 3)
                hidden(i, pp, j, 2)
                hidden(i, pp, j, 3)
                if outputs:
                    output(i, pp - 1, j * HC, range(CK))
                if ahead:
                    turn(i, pp, j + 1, 0)
                if outputs:
                    output(i, pp - 1, j * HC + 1, range(CK // 2))
                if ahead:
                    turn(i, pp, j + 1, 1)
                if outputs:
                    output(i, pp - 1, j * HC + 1, range(CK // 2, CK))

            def rest(i, pp):
                for c in range(NC):
                    output(i, pp, c, range(CK))

            pipeline(e, part, rest)

        @block.scalar
        def _(e):
            e.sem_inc(gelu_done, 1)

            def split_u(i, pp, j, c):
                pp, j = pp + j // 2, j % 2
                e.wait_ge(u_turned, at(i, pp, 2 * NC, j * NC + c + 5))
                e.wait_ge(uT_used, at(i, pp, 2 * NC, j * NC + c + 1))
                e.activation(uT[:, c, 0], tp[:, c % 2], ACT.Copy).then_inc(uT_hi, 1)

            def split_v(i, pp, c):
                e.wait_ge(v_in[c % 2], at(i, pp, 32, 16 * (c // 2 + 1)))
                e.wait_ge(y_ready, at(i, pp, KT, CK * c + KT - CK))
                e.activation(v[:, c % 2, 0], v_raw[:, c % 2], ACT.Copy).then_inc(v_hi, 1)

            def part(i, pp, j, outputs, ahead):
                if not outputs and j == 0:
                    split_u(i, pp, j, 0)
                    split_u(i, pp, j, 1)
                if outputs:
                    split_v(i, pp - 1, j * HC)
                split_u(i, pp, j, 2)
                if outputs:
                    split_v(i, pp - 1, j * HC + 1)
                split_u(i, pp, j, 3)
                e.wait_ge(uT_used, at(i, pp, 2 * NC, (j + 1) * NC + 4))
                e.wait_ge(w_rest, at(i, pp, 2, j + 1))
                e.activation(halves(hid[:, j, :]), h_ps[:, :, 0:HALF], ACT.Gelu_apprx_tanh).then_inc(gelu_done, 1)
                e.wait_ge(gated, at(i, pp, 2, j + 4))
                if outputs:
                    e.wait_ge(y_ready, at(i, pp, KT, 0))
                e.activation(wt[:, pp % 2, j, 0, :], hid[:, j, :], ACT.Copy).then_inc(w_hi, 1)
                if ahead:
                    split_u(i, pp, j + 1, 0)
                    split_u(i, pp, j + 1, 1)

            def rest(i, pp):
                for c in range(NC):
                    split_v(i, pp, c)

            pipeline(e, part, rest)

        @block.gpsimd
        def _(e):
            e.sem_inc(v_rest, 2)

            def split_v(i, pp, c):
                e.wait_ge(v_hi, at(i, pp, NC, c + 1))
                e.tensor_tensor(v[:, c % 2, 1], v_raw[:, c % 2], v[:, c % 2, 0].bitcast(F32),
                                ALU.subtract).then_inc(v_rest, 1)

            def part(i, pp, j, outputs, ahead):
                if outputs:
                    for c in range(HC):
                        split_v(i, pp - 1, j * HC + c)

            def rest(i, pp):
                for c in range(NC):
                    split_v(i, pp, c)

            pipeline(e, part, rest)

        @block.vector
        def _(e):
            e.sem_inc(uT_rest, 2)
            e.sem_inc(gated, 3)
            e.sem_inc(w_rest, 2)
            e.sem_inc(y_added, 2)

            def split_u(i, pp, j, c):
                pp, j = pp + j // 2, j % 2
                e.wait_ge(uT_hi, at(i, pp, 2 * NC, j * NC + c + 1))
                e.tensor_tensor(uT[:, c, 1], tp[:, c % 2], uT[:, c, 0].bitcast(F32), ALU.subtract).then_inc(uT_rest, 1)

            def add(i, pp, c, tiles):
                for t in tiles:
                    e.wait_ge(y_ready, at(i, pp, KT, c * CK + t + 1 + KT))
                    x = halves(k.xT[:, c * CK + t, :])
                    e.tensor_tensor(x, x, y_ps[:, t % 2, :, 0:HALF], ALU.add).then_inc(y_added, 1)

            def part(i, pp, j, outputs, ahead):
                if not outputs and j == 0:
                    split_u(i, pp, j, 0)
                    split_u(i, pp, j, 1)
                split_u(i, pp, j, 2)
                split_u(i, pp, j, 3)
                if j == 0:
                    e.wait_ge(gate_in[pp % 2], i * 16 + 16 * (pp // 2 + 1))
                e.wait_ge(gelu_done, at(i, pp, 2, j + 2))
                e.tensor_tensor(hid[:, j, :], hid[:, j, :], gate[:, pp % 2, j, :], ALU.mult).then_inc(gated, 1)
                if outputs:
                    add(i, pp - 1, j * HC, range(1))
                e.wait_ge(w_hi, at(i, pp, 2, j + 1))
                e.tensor_tensor(wt[:, pp % 2, j, 1, :], hid[:, j, :], wt[:, pp % 2, j, 0, :].bitcast(F32),
                                ALU.subtract).then_inc(w_rest, 1)
                if outputs:
                    add(i, pp - 1, j * HC, range(1, CK))
                if ahead:
                    split_u(i, pp, j + 1, 0)
                if outputs:
                    add(i, pp - 1, j * HC + 1, range(CK // 2))
                if ahead:
                    split_u(i, pp, j + 1, 1)
                if outputs:
                    add(i, pp - 1, j * HC + 1, range(CK // 2, CK))

            def rest(i, pp):
                for c in range(NC):
                    add(i, pp, c, range(CK))

            pipeline(e, part, rest)


def stage_ple(k):
    nc = k.nc
    with Space(nc, "ple") as s:
        w = Stream(s)
        p_rows = s.sb("p_rows", [P, TB, PLE])
        pT = s.sb("pT", [P, 2, TOK])
        ps_ = s.sb("ps", [P, 2, 2, TOK], F32R)
        sig = s.sb("sig", [P, TOK])
        part = s.sb("part", [P, TOK])
        x3 = s.sb("x3", [P, 2, TOK])
        rows = s.sb("rows", [P, 2, TB, P])
        acc = [s.ps(f"acc{a}", [P, 2, 512]) for a in range(2)]
        emb = s.ps("emb", [P, 2, 512])
        tp = s.ps("tp", [P, 2, 512])
        p_in, p_turned, p_ready, p_hi, p_rest = (s.sem(x) for x in ("p_in", "p_turned", "p_ready", "p_hi", "p_rest"))
        acc_free, emb_free, sig_used, x3_ready, x3_used, tp_free, rows_ready = (
            s.sem(x) for x in ("acc_free", "emb_free", "sig_used", "x3_ready", "x3_used", "tp_free", "rows_ready"))
        stored = s.sems("stored", 2)
        chain_sem = s.sem("chain")
        block = s.block()
        U = KT // UNIT
        PC = U + 1
        BC = 4
        PER = BC * PC
        N = KT // BC

        @block.sync
        def _(e):
            e.dma_start(p_rows[:, 0:4, :], k.p_prompt[0, 0].rearrange("(b p) c -> p b c", p=P)).then_inc(p_in, 16)
            e.dma_start(p_rows[0:NS, 4, :], k.p_sample[0].rearrange("b t c -> (b t) c")).then_inc(p_in, 16)
            with e.Fori(0, N) as i:
                for a in range(BC):
                    col = i * (BC * P) + a * P
                    for u in range(U):
                        w.load(e, i, PER, a * PC + u, columns(k.w_ple_gate[0], col, UNIT * u))
                    w.load(e, i, PER, a * PC + U, columns(k.w_ple[0], col, 0, 2))

        @block.gpsimd
        def _(e):
            w.credit_rest(e)
            with e.Fori(0, N) as i:
                for a in range(BC):
                    for u in range(PC):
                        w.split_rest(e, i, PER, a * PC + u, UNIT if u < U else 2)

        @block.scalar
        def _(e):
            e.wait_ge(p_ready, 2)
            e.activation(ps_[:, :, 0, :], pT[:], ACT.Copy).then_inc(p_hi, 1)
            e.sem_inc(acc_free, 2)
            e.sem_inc(tp_free, 1)
            e.sem_inc(stored[0], 32)
            e.sem_inc(stored[1], 32)

            def sigmoid(i, a):
                w.wait_used(e, i, PER, (a + 1) * PC)
                e.wait_ge(sig_used, i * BC + (a + 1))
                e.activation(halves(sig[:]), acc[a % 2][:, :, 0:HALF], ACT.Sigmoid).then_inc(acc_free, 1)

            def rows_out(i, a):
                e.wait_ge(x3_used, i * BC + (a + 3))
                e.wait_ge(stored[a % 2], i * (32 * BC // 2) + 32 * (a // 2 + 1))
                e.activation(rows[:, a % 2, 0:4, :], tp[:, 0, :].rearrange("p (b n) -> p b n", b=4), ACT.Copy)
                e.activation(rows[0:NS, a % 2, 4, :], tp[0:NS, 1, 0:P], ACT.Copy).then_inc(tp_free, 1)
                e.wait_ge(tp_free, i * BC + (a + 2))
                col = i * (BC * P) + a * P
                e.dma_start(k.y_prompt[0].rearrange("(b p) d -> p b d", p=P)[:, :, ds(col, P)],
                            rows[:, a % 2, 0:4, :]).then_inc(stored[a % 2], 16)
                e.dma_start(k.y_sample.rearrange("b t d -> (b t) d")[:, ds(col, P)],
                            rows[0:NS, a % 2, 4, :]).then_inc(stored[a % 2], 16)

            def body(i, first):
                for a in range(BC):
                    for u in range(PC):
                        w.split_hi(e, i, PER, a * PC + u, UNIT if u < U else 2)
                        if u == 3:
                            if a:
                                sigmoid(i, a - 1)
                            elif not first:
                                sigmoid(i - 1, BC - 1)
                    if a >= 3:
                        rows_out(i, a - 3)
                    elif not first:
                        rows_out(i - 1, BC - 3 + a)

            body(0, True)
            with e.Fori(1, N) as i:
                body(i, False)
            sigmoid(N - 1, BC - 1)
            for a in range(BC - 3, BC):
                rows_out(N - 1, a)
            for a in range(2):
                e.wait_ge(stored[a], 32 * (KT // 2 + 1))

        @block.tensor
        def _(e):
            w.credit_used(e)
            e.sem_inc(x3_used, 2)
            e.wait_ge(p_in, 32)
            for t in range(2):
                if t:
                    e.wait_ge(p_ready, 1)
                for b in range(TB):
                    n = P if b < 4 else NS
                    mm = e.transpose(tp[:, b // 4, (b % 4) * P:(b % 4) * P + n], p_rows[0:n, b, t * P:(t + 1) * P],
                                     k.c("ident")[0:n, 0:n])
                mm.then_inc(p_turned, 1)
            e.wait_ge(p_rest, 1)

            def turn(i, a):
                e.wait_ge(x3_ready, i * BC + (a + 1))
                e.wait_ge(tp_free, i * BC + (a + 1))
                for b in range(TB):
                    n = P if b < 4 else NS
                    mm = e.transpose(tp[0:n, b // 4, (b % 4) * P:(b % 4 + 1) * P], x3[:, a % 2, b * P:b * P + n],
                                     k.c("ident"))
                mm.then_inc(x3_used, 1)

            def body(i, first):
                for a in range(BC):
                    e.wait_ge(acc_free, i * BC + (a + 1))
                    for u in range(U):
                        w.multiply(e, i, PER, a * PC + u, acc[a % 2], k.act, u * UNIT, u == 0, u == U - 1)
                    e.wait_ge(emb_free, i * BC + (a + 1))
                    w.multiply(e, i, PER, a * PC + U, emb, ps_, 0, True, True, 2)
                    if a >= 2:
                        turn(i, a - 2)
                    elif not first:
                        turn(i - 1, BC - 2 + a)

            body(0, True)
            with e.Fori(1, N) as i:
                body(i, False)
            turn(N - 1, BC - 2)
            turn(N - 1, BC - 1)

        @block.vector
        def _(e):
            ch = Chain(e, chain_sem)
            for t in range(2):
                e.wait_ge(p_turned, t + 1)
                ch.did(e.tensor_copy(pT[:, t, 0:NP], tp[:, 0, :]))
                e.tensor_copy(pT[:, t, NP:TOK], tp[:, 1, 0:NS]).then_inc(p_ready, 1)
            ch.wait()
            e.wait_ge(p_hi, 1)
            e.tensor_tensor(ps_[:, :, 1, :], pT[:], ps_[:, :, 0, :].bitcast(F32), ALU.subtract).then_inc(p_rest, 1)
            e.sem_inc(emb_free, 1)
            e.sem_inc(sig_used, 1)
            with e.Fori(0, N) as i:
                ch.begin(i, BC)
                for a in range(BC):
                    e.wait_ge(acc_free, i * BC + (a + 3))
                    ch.step(e.tensor_tensor(halves(part[:]), emb[:, :, 0:HALF], halves(sig[:]), ALU.mult))
                    e.sem_inc(emb_free, 1)
                    e.sem_inc(sig_used, 1)
                    e.wait_ge(x3_used, i * BC + (a + 1))
                    e.tensor_tensor(x3[:, a % 2, :], part[:], k.xT[:, ds(i * BC + a, 1), :].rearrange("p o n -> p (o n)"),
                                    ALU.add).then_inc(x3_ready, 1)
                    e.wait_ge(x3_ready, i * BC + (a + 1))
            ch.end(N)


class Kernel:

    def c(self, name):
        a, w = CONST_AT[name]
        return self.const[:, a:a + w]


def build(nc, ins, outs, stages=99):
    k = Kernel()
    k.nc = nc
    k.x_prompt = ins["x_prompt"]
    k.x_sample = ins["x_sample"]
    k.cache_k = ins["cache_k"]
    k.cache_v = ins["cache_v"]
    k.state_ssm_re = ins["state_ssm_re"]
    k.state_ssm_im = ins["state_ssm_im"]
    k.page_table = ins["page_table"]
    k.p_prompt = ins["p_prompt"]
    k.p_sample = ins["p_sample"]
    k.g_mix = ins["g_mix"]
    k.w_in = ins["w_in"]
    k.g_q = ins["g_q"]
    k.g_k = ins["g_k"]
    k.lambda_q = ins["lambda_q"]
    k.lambda_k = ins["lambda_k"]
    k.g_head = ins["g_head"]
    k.w_attn_up = ins["w_attn_up"]
    k.ssm_a_re = ins["ssm_a_re"]
    k.ssm_a_im = ins["ssm_a_im"]
    k.ssm_log_dt = ins["ssm_log_dt"]
    k.ssm_b_re = ins["ssm_b_re"]
    k.ssm_b_im = ins["ssm_b_im"]
    k.ssm_c_re = ins["ssm_c_re"]
    k.ssm_c_im = ins["ssm_c_im"]
    k.ssm_d = ins["ssm_d"]
    k.w_glu = ins["w_glu"]
    k.w_out = ins["w_out"]
    k.g_ffn = ins["g_ffn"]
    k.peer_w_query = ins["peer_w_query"]
    k.peer_sub_keys = ins["peer_sub_keys"]
    k.peer_u = ins["peer_u"]
    k.peer_v = ins["peer_v"]
    k.g_ple = ins["g_ple"]
    k.w_ple = ins["w_ple"]
    k.w_ple_gate = ins["w_ple_gate"]
    k.const_dram = ins["const_dram"]
    (k.y_prompt, k.y_sample, k.new_k_prompt, k.new_v_prompt, ssm_re_p, ssm_im_p,
     k.new_k_sample, k.new_v_sample, ssm_re_s, ssm_im_s) = outs
    k.new_ssm_prompt, k.new_ssm_sample = (ssm_re_p, ssm_im_p), (ssm_re_s, ssm_im_s)
    k.xT_dram = nc.dram_tensor("xT_scratch", [P, KT, TOK], F32).ap()
    k.z_dram = nc.dram_tensor("z_scratch", [56, P, TOK], F32).ap()
    k.y_dram = nc.dram_tensor("y_scratch", [CT, P, TOK], F32).ap()
    k.mix_dram = nc.dram_tensor("mix_scratch", [KT, P, TOK], F32).ap()
    k.gate_dram = nc.dram_tensor("gate_scratch", [P, PK, TOK], F32).ap()
    with Space(nc, "all") as s:
        k.const = s.sb("const", [P, CONST_W])
        with Space(nc, "in") as s1:
            k.act = s1.sb("act", [P, KT, 2, TOK], F32R)
            stage_prepare(k)
            k.uT = s1.sb("uT", [P, CT, TOK])
            k.tw_lo = s1.sb("tw_lo", [P, 2, ST, LO])
            k.tw_hi = s1.sb("tw_hi", [P, 2, ST, HI])
            k.mag = s1.sb("mag", [P, ST])
            k.ab = s1.sb("ab", [P, 2, ST])
            k.BT = s1.sb("BT", [P, 2, CT, P])
            k.CTm = s1.sb("CTm", [P, 2, ST, 2 * GC])
            k.ssm_d_col = s1.sb("ssm_d_col", [P, CT])
            k.fin = s1.sb("fin", [P, 2, ST])
            if stages < 2: return k
            stage_ssm_input(k)
            if stages < 3: return k
            stage_scan(k)
            if stages < 4: return k
            stage_scan_sample(k)
        if stages < 5: return k
        with Space(nc, "heads") as s2:
            k.o = s2.sb("o", [P, NH, TOK])
            k.qk_sample = s2.sb("qk_sample", [P, 2, NH, NS])
            k.neg_lam = s2.sb("neg_lam", [P, 1])
            stage_attention_prompt(k)
            stage_attention_sample(k)
            k.att = s2.sb("att", [P, NH, 2, TOK], F32R)
            stage_attention_norm(k)
            if stages < 6: return k
            stage_mix(k)
        if stages < 7: return k
        with Space(nc, "out") as s4:
            k.xT = s4.sb("xT", [P, KT, TOK])
            k.act = s4.sb("act", [P, KT, 2, TOK], F32R)
            stage_out(k)
            if stages < 8: return k
            stage_norm(k, k.g_ffn[0], "nffn")
            with Space(nc, "picks") as s5:
                k.tables = s5.sb("tables", [P, 3, TOK])
                with Space(nc, "ranks") as s6:
                    k.idx = s6.sb("idx", [P, TB, NH, 2 * TOPK])
                    k.best = s6.sb("best", [P, TB, NH, TOPK])
                    k.at = s6.sb("at", [P, TB, NH, TOPK], U32)
                    stage_route(k)
                    stage_tables(k)
                stage_gates(k)
            if stages < 10: return k
            stage_experts(k)
            if stages < 11: return k
            stage_norm(k, k.g_ple[0], "nple")
            stage_ple(k)
    return k


_INS = ["x_prompt", "x_sample", "cache_k", "cache_v", "state_ssm_re", "state_ssm_im", "page_table", "p_prompt",
        "p_sample", "g_mix", "w_in", "g_q", "g_k", "lambda_q", "lambda_k", "g_head", "w_attn_up", "ssm_a_re",
        "ssm_a_im", "ssm_log_dt", "ssm_b_re", "ssm_b_im", "ssm_c_re", "ssm_c_im", "ssm_d", "w_glu", "w_out", "g_ffn",
        "peer_w_query", "peer_sub_keys", "peer_u", "peer_v", "g_ple", "w_ple", "w_ple_gate"]
_OUTS = [(1, NP, D_MODEL), (NB, NQ, D_MODEL), (1, 1, NP, NH, 2 * DK), (1, 1, NP, NH, DV), (1, 1, G, GS), (1, 1, G, GS),
         (1, NB, NQ, NH, 2 * DK), (1, NB, NQ, NH, DV), (1, NB, G, GS), (1, NB, G, GS)]


def kernel(**inputs):
    import concourse.bacc as bacc
    from concourse.bass_utils import run_bass_kernel_spmd

    nc = bacc.Bacc("TRN2", target_bir_lowering=False, num_devices=1)
    arrays, ins = {}, {}
    for name in _INS:
        a = np.ascontiguousarray(inputs[name])
        arrays[f"in_{name}"] = a
        ins[name] = nc.dram_tensor(f"in_{name}", a.shape, mybir.dt.from_np(a.dtype), kind="ExternalInput").ap()
    arrays["in_const"] = shape_constants()
    ins["const_dram"] = nc.dram_tensor("in_const", (P, CONST_W), F32, kind="ExternalInput").ap()
    outs = [nc.dram_tensor(f"out_{n}", shape, F32, kind="ExternalOutput").ap() for n, shape in enumerate(_OUTS)]
    build(nc, ins, outs)
    r = run_bass_kernel_spmd(nc, [arrays], core_ids=[0])
    return tuple(r.results[0][f"out_{n}"] for n in range(len(_OUTS)))
```
